# Optimizing a Trainium2 kernel written in Bass

```python
import jax, jax.numpy as jnp
from jax import lax
import numpy as np
import math

D_MODEL = 2048
BATCH = 1
SEQ = 256
DEPTH = 1

D_MIX = D_MODEL
D_POOL = D_MIX // 2
POOL_WINDOWS = (2, 4, 8, 16)
N_POOL_GROUPS = len(POOL_WINDOWS)
POOL_GROUP_DIM = D_POOL // N_POOL_GROUPS
D_GLA = D_MIX - D_POOL
GLA_HEADS = 4
GLA_DV = D_GLA // GLA_HEADS
GLA_DK_TOTAL = D_GLA // 2
GLA_DK = GLA_DK_TOTAL // GLA_HEADS
GLA_GATE_RANK = 16
GATE_LOGIT_NORMALIZER = 16.0
CHUNK = 64
D_IN = D_POOL + 2 * GLA_DK_TOTAL + 2 * D_GLA + GLA_GATE_RANK
D_FF = 5632
EPS = 1e-6


def rmsnorm(x, g):
    xf = x.astype(jnp.float32)
    y = xf * lax.rsqrt(jnp.mean(xf * xf, axis=-1, keepdims=True) + EPS)
    return (y * g.astype(jnp.float32)).astype(x.dtype)

def swiglu(h, w_in, w_out):
    gu = h @ w_in
    gate, up = gu[..., :D_FF], gu[..., D_FF:]
    return (jax.nn.silu(gate) * up) @ w_out

def pool_mixer(u, w_pool, pool_scale):
    B, S, _ = u.shape
    uf = u.astype(jnp.float32).reshape(B, S, N_POOL_GROUPS, POOL_GROUP_DIM)
    cs = jnp.cumsum(uf, axis=1)
    pos1 = jnp.arange(1, S + 1, dtype=jnp.int32)
    means = []
    for gi, w in enumerate(POOL_WINDOWS):
        c = cs[:, :, gi]
        shifted = jnp.pad(c, ((0, 0), (w, 0), (0, 0)))[:, :S]
        cnt = jnp.minimum(pos1, w).astype(jnp.float32)[None, :, None]
        means.append((c - shifted) / cnt)
    pooled = jnp.stack(means, axis=2) - uf
    y = jnp.einsum('bsgc,gcd->bsgd', pooled.astype(u.dtype), w_pool)
    return y.reshape(B, S, D_POOL) * pool_scale

def gla_mixer(q, k, v, g_out, gate_lr, w_alpha, b_alpha, gla_norm):
    B, S, _ = q.shape
    N = S // CHUNK
    log_alpha = jax.nn.log_sigmoid((gate_lr @ w_alpha + b_alpha).astype(jnp.float32)) / GATE_LOGIT_NORMALIZER

    def heads(t, d):
        return t.astype(jnp.float32).reshape(B, N, CHUNK, GLA_HEADS, d).transpose(0, 3, 1, 2, 4)

    qh = heads(q, GLA_DK) * (GLA_DK ** -0.5)
    kh = heads(k, GLA_DK)
    vh = heads(v, GLA_DV)
    bcum = jnp.cumsum(heads(log_alpha, GLA_DK), axis=3)
    b_last = bcum[:, :, :, -1:]
    q_dec = qh * jnp.exp(bcum)
    k_inv = kh * jnp.exp(-bcum)
    k_tail = kh * jnp.exp(b_last - bcum)

    mask = jnp.tril(jnp.ones((CHUNK, CHUNK), dtype=bool))
    scores = jnp.where(mask, jnp.einsum('bhnid,bhnjd->bhnij', q_dec, k_inv), 0.0)
    o_intra = jnp.einsum('bhnij,bhnjv->bhniv', scores, vh)

    kv_chunk = jnp.einsum('bhncd,bhncv->bhndv', k_tail, vh)
    decay_chunk = jnp.exp(b_last[:, :, :, 0])

    def step(state, inp):
        dec, kv = inp
        return state * dec[..., None] + kv, state

    init = jnp.zeros((B, GLA_HEADS, GLA_DK, GLA_DV), jnp.float32)
    _, states = lax.scan(step, init, (decay_chunk.transpose(2, 0, 1, 3), kv_chunk.transpose(2, 0, 1, 3, 4)))
    states = states.transpose(1, 2, 0, 3, 4)
    o = o_intra + jnp.einsum('bhncd,bhndv->bhncv', q_dec, states)

    o = o * lax.rsqrt(jnp.mean(o * o, axis=-1, keepdims=True) + EPS) * gla_norm.astype(jnp.float32)
    o = o.transpose(0, 2, 3, 1, 4).reshape(B, S, D_GLA)
    return (o * jax.nn.silu(g_out.astype(jnp.float32))).astype(q.dtype)

def first_inputs(seed: int = 0) -> dict:
    key = jax.random.key(seed)
    ks = jax.random.split(key, 16)
    f32 = jnp.float32

    def nrm(k, shape, fan_in):
        return jax.random.normal(k, shape, f32) * (fan_in ** -0.5)

    def gain(k, shape):
        return 1.0 + 0.02 * jax.random.normal(k, shape, f32)

    L = DEPTH
    return {
        "x": jax.random.normal(ks[0], (BATCH, SEQ, D_MODEL), f32),
        "ffn1_norm": gain(ks[1], (L, D_MODEL)),
        "ffn1_w_in": nrm(ks[2], (L, D_MODEL, 2 * D_FF), D_MODEL),
        "ffn1_w_out": nrm(ks[3], (L, D_FF, D_MODEL), D_FF),
        "mix_norm": gain(ks[4], (L, D_MODEL)),
        "w_in_mix": nrm(ks[5], (L, D_MODEL, D_IN), D_MODEL),
        "w_pool": nrm(ks[6], (L, N_POOL_GROUPS, POOL_GROUP_DIM, POOL_GROUP_DIM), POOL_GROUP_DIM),
        "pool_scale": 1.0 + 0.1 * jax.random.normal(ks[7], (L, D_POOL), f32),
        "w_alpha": nrm(ks[8], (L, GLA_GATE_RANK, GLA_DK_TOTAL), GLA_GATE_RANK),
        "b_alpha": 0.01 * jax.random.normal(ks[9], (L, GLA_DK_TOTAL), f32),
        "gla_norm": gain(ks[10], (L, GLA_DV)),
        "w_out_mix": nrm(ks[11], (L, D_MIX, D_MODEL), D_MIX),
        "ffn2_norm": gain(ks[12], (L, D_MODEL)),
        "ffn2_w_in": nrm(ks[13], (L, D_MODEL, 2 * D_FF), D_MODEL),
        "ffn2_w_out": nrm(ks[14], (L, D_FF, D_MODEL), D_FF),
        "final_norm": gain(ks[15], (D_MODEL,)),
    }

def first_block(x, ffn1_norm, ffn1_w_in, ffn1_w_out, mix_norm, w_in_mix, w_pool, pool_scale,
              w_alpha, b_alpha, gla_norm, w_out_mix, ffn2_norm, ffn2_w_in, ffn2_w_out, final_norm):
    h = x
    o_q = D_POOL
    o_k = o_q + GLA_DK_TOTAL
    o_v = o_k + GLA_DK_TOTAL
    o_g = o_v + D_GLA
    o_r = o_g + D_GLA
    for l in range(DEPTH):
        h = h + 0.5 * swiglu(rmsnorm(h, ffn1_norm[l]), ffn1_w_in[l], ffn1_w_out[l])
        u = rmsnorm(h, mix_norm[l]) @ w_in_mix[l]
        y_pool = pool_mixer(u[..., :o_q], w_pool[l], pool_scale[l])
        y_gla = gla_mixer(u[..., o_q:o_k], u[..., o_k:o_v], u[..., o_v:o_g], u[..., o_g:o_r],
                          u[..., o_r:], w_alpha[l], b_alpha[l], gla_norm[l])
        h = h + jnp.concatenate([y_pool.astype(h.dtype), y_gla.astype(h.dtype)], axis=-1) @ w_out_mix[l]
        h = h + 0.5 * swiglu(rmsnorm(h, ffn2_norm[l]), ffn2_w_in[l], ffn2_w_out[l])
    return rmsnorm(h, final_norm)


DEPTH_2 = 2

HEAD_DIM = 128
N_HEADS_A = D_MODEL // HEAD_DIM
N_KV_A = 4
ROT_DIM = HEAD_DIM // 4
IDX_HEADS = 16
IDX_DIM = 64
IDX_ROT = IDX_DIM // 4
TOPK_MAX = 256
N_HEADS_B = D_MODEL // HEAD_DIM
N_KV_B = 4
BLOCK_Q = 128
PLE_DIM = 256
ROPE_THETA = 500000.0
LN_EPS = 1e-5
N_A_LAYERS = DEPTH_2 // 2
N_B_LAYERS = DEPTH_2 - N_A_LAYERS
ALPHA = (2.0 * DEPTH_2) ** 0.25
BETA = (8.0 * DEPTH_2) ** -0.25

WIDTH_A = N_HEADS_A * HEAD_DIM
KVW_A = N_KV_A * HEAD_DIM
SPLITS_A = tuple(int(c) for c in np.cumsum([WIDTH_A, KVW_A, KVW_A, WIDTH_A, IDX_HEADS * IDX_DIM, IDX_DIM]))
COLS_A = WIDTH_A + 2 * KVW_A + WIDTH_A + IDX_HEADS * IDX_DIM + IDX_DIM + IDX_HEADS
WIDTH_B = N_HEADS_B * HEAD_DIM
KVW_B = N_KV_B * HEAD_DIM


def layer_norm(x, g, b):
    xf = x.astype(jnp.float32)
    mu = jnp.mean(xf, axis=-1, keepdims=True)
    var = jnp.mean(jnp.square(xf - mu), axis=-1, keepdims=True)
    y = (xf - mu) * lax.rsqrt(var + LN_EPS) * g.astype(jnp.float32) + b.astype(jnp.float32)
    return y.astype(x.dtype)

def partial_rope(x, positions, rot_dim):
    half = rot_dim // 2
    inv = 1.0 / (ROPE_THETA ** (jnp.arange(half, dtype=jnp.float32) / half))
    ang = positions.astype(jnp.float32)[..., None] * inv
    cos = jnp.cos(ang)[:, :, None, :]
    sin = jnp.sin(ang)[:, :, None, :]
    xr = x[..., :rot_dim].astype(jnp.float32)
    x1, x2 = xr[..., :half], xr[..., half:]
    rot = jnp.concatenate([x1 * cos - x2 * sin, x1 * sin + x2 * cos], axis=-1)
    return jnp.concatenate([rot.astype(x.dtype), x[..., rot_dim:]], axis=-1)

def to_blocks(a):
    b, s = a.shape[0], a.shape[1]
    return jnp.swapaxes(a.reshape((b, s // BLOCK_Q, BLOCK_Q) + a.shape[2:]), 0, 1)

def from_blocks(a):
    a = jnp.swapaxes(a, 0, 1)
    return a.reshape((a.shape[0], a.shape[1] * a.shape[2]) + a.shape[3:])

def mixer_a(x, w_in, w_o, positions):
    b, s, _ = x.shape
    proj = x @ w_in
    q, k, v, gate, iq, ik, iw = jnp.split(proj, SPLITS_A, axis=-1)
    q = partial_rope(q.reshape(b, s, N_HEADS_A, HEAD_DIM), positions, ROT_DIM)
    k = partial_rope(k.reshape(b, s, N_KV_A, HEAD_DIM), positions, ROT_DIM)
    v = v.reshape(b, s, N_KV_A, HEAD_DIM)
    iq = partial_rope(iq.reshape(b, s, IDX_HEADS, IDX_DIM), positions, IDX_ROT)
    ik = partial_rope(ik.reshape(b, s, 1, IDX_DIM), positions, IDX_ROT)[:, :, 0, :]
    n_sel = min(TOPK_MAX, s // 4)
    groups = N_HEADS_A // N_KV_A
    key_pos = jnp.arange(s, dtype=jnp.int32)
    idx_scale = (IDX_DIM ** -0.5) * (IDX_HEADS ** -0.5)
    starts = jnp.arange(s // BLOCK_Q, dtype=jnp.int32) * BLOCK_Q

    def block_fn(args):
        qb, iqb, iwb, start = args
        t = start + jnp.arange(BLOCK_Q, dtype=jnp.int32)
        dots = jnp.einsum('bqhd,bsd->bqhs', iqb, ik).astype(jnp.float32)
        iscore = jnp.einsum('bqhs,bqh->bqs', jax.nn.relu(dots), iwb.astype(jnp.float32)) * idx_scale
        causal = key_pos[None, :] <= t[:, None]
        iscore = jnp.where(causal[None], iscore, -jnp.inf)
        _, idx = lax.top_k(iscore, n_sel)
        ksel = jax.vmap(lambda kk, ii: kk[ii])(k, idx)
        vsel = jax.vmap(lambda vv, ii: vv[ii])(v, idx)
        qg = qb.reshape(b, BLOCK_Q, N_KV_A, groups, HEAD_DIM)
        logits = jnp.einsum('bqngd,bqknd->bqngk', qg, ksel).astype(jnp.float32) * (HEAD_DIM ** -0.5)
        valid = idx <= t[None, :, None]
        logits = jnp.where(valid[:, :, None, None, :], logits, -jnp.inf)
        wts = jax.nn.softmax(logits, axis=-1).astype(v.dtype)
        o = jnp.einsum('bqngk,bqknd->bqngd', wts, vsel)
        return o.reshape(b, BLOCK_Q, WIDTH_A)

    o = from_blocks(lax.map(block_fn, (to_blocks(q), to_blocks(iq), to_blocks(iw), starts)))
    return (o * jax.nn.silu(gate)) @ w_o

def shared_kv(x, w_kv):
    b, s, _ = x.shape
    k, v = jnp.split(x @ w_kv, [KVW_B], axis=-1)
    return k.reshape(b, s, N_KV_B, HEAD_DIM), v.reshape(b, s, N_KV_B, HEAD_DIM)

def mixer_b(x, w_in, w_o, k, v):
    b, s, _ = x.shape
    q, gate = jnp.split(x @ w_in, [WIDTH_B], axis=-1)
    q = q.reshape(b, s, N_HEADS_B, HEAD_DIM)
    groups = N_HEADS_B // N_KV_B
    key_pos = jnp.arange(s, dtype=jnp.int32)
    starts = jnp.arange(s // BLOCK_Q, dtype=jnp.int32) * BLOCK_Q

    def block_fn(args):
        qb, start = args
        t = start + jnp.arange(BLOCK_Q, dtype=jnp.int32)
        qg = qb.reshape(b, BLOCK_Q, N_KV_B, groups, HEAD_DIM)
        z = jnp.einsum('bqngd,bsnd->bngqs', qg, k).astype(jnp.float32) * (HEAD_DIM ** -0.5)
        strict = key_pos[None, :] < t[:, None]
        log_om = jnp.where(strict, -jax.nn.softplus(z), 0.0)
        suffix = lax.cumsum(log_om, axis=log_om.ndim - 1, reverse=True) - log_om
        a = jnp.where(strict, jnp.exp(jax.nn.log_sigmoid(z) + suffix), 0.0)
        o = jnp.einsum('bngqs,bsnd->bqngd', a.astype(v.dtype), v)
        return o.reshape(b, BLOCK_Q, WIDTH_B)

    o = from_blocks(lax.map(block_fn, (to_blocks(q), starts)))
    return (o * jax.nn.silu(gate)) @ w_o

def per_layer_embed(x, p_i, w_p, w_g):
    return (p_i @ w_p) * jax.nn.sigmoid(x @ w_g)

def second_inputs(seed: int = 0) -> dict:
    key = jax.random.key(seed)
    ks = jax.random.split(key, 12)
    nrm = jax.random.normal
    x = nrm(ks[0], (BATCH, SEQ, D_MODEL), jnp.float32)
    p = nrm(ks[1], (DEPTH_2, BATCH, SEQ, PLE_DIM), jnp.float32)
    positions = jnp.broadcast_to(jnp.arange(SEQ, dtype=jnp.int32)[None, :], (BATCH, SEQ))
    w_in_a = nrm(ks[2], (N_A_LAYERS, D_MODEL, COLS_A), jnp.float32) * D_MODEL ** -0.5
    w_o_a = nrm(ks[3], (N_A_LAYERS, WIDTH_A, D_MODEL), jnp.float32) * (WIDTH_A ** -0.5 * BETA)
    w_kv_b = nrm(ks[4], (D_MODEL, 2 * KVW_B), jnp.float32) * D_MODEL ** -0.5
    w_in_b = nrm(ks[5], (N_B_LAYERS, D_MODEL, 2 * WIDTH_B), jnp.float32) * D_MODEL ** -0.5
    w_o_b = nrm(ks[6], (N_B_LAYERS, WIDTH_B, D_MODEL), jnp.float32) * (WIDTH_B ** -0.5 * BETA)
    ln_g = 1.0 + 0.02 * nrm(ks[7], (DEPTH_2, D_MODEL), jnp.float32)
    ln_b = 0.02 * nrm(ks[8], (DEPTH_2, D_MODEL), jnp.float32)
    w_ple = nrm(ks[9], (DEPTH_2, PLE_DIM, D_MODEL), jnp.float32) * PLE_DIM ** -0.5
    w_ple_gate = nrm(ks[10], (DEPTH_2, D_MODEL, D_MODEL), jnp.float32) * D_MODEL ** -0.5
    return {"x": x, "p": p, "positions": positions, "w_in_a": w_in_a, "w_o_a": w_o_a,
            "w_kv_b": w_kv_b, "w_in_b": w_in_b, "w_o_b": w_o_b, "ln_g": ln_g, "ln_b": ln_b,
            "w_ple": w_ple, "w_ple_gate": w_ple_gate}

def second_block(x, p, positions, w_in_a, w_o_a, w_kv_b, w_in_b, w_o_b, ln_g, ln_b, w_ple, w_ple_gate):
    k_sh, v_sh = None, None
    for i in range(DEPTH_2):
        if i < N_A_LAYERS:
            h = mixer_a(x, w_in_a[i], w_o_a[i], positions)
        else:
            if i == N_A_LAYERS:
                k_sh, v_sh = shared_kv(x, w_kv_b)
            j = i - N_A_LAYERS
            h = mixer_b(x, w_in_b[j], w_o_b[j], k_sh, v_sh)
        x = layer_norm(ALPHA * x + h, ln_g[i], ln_b[i])
        x = x + per_layer_embed(x, p[i], w_ple[i], w_ple_gate[i])
    return x


def setup_inputs(seed=0):
    out = dict(first_inputs(seed))
    for name, value in second_inputs(seed + 1).items():
        if name != "x":
            out[name + "_2"] = value
    return out


def reference(
    x, ffn1_norm, ffn1_w_in, ffn1_w_out, mix_norm, w_in_mix, w_pool, pool_scale, w_alpha,
    b_alpha, gla_norm, w_out_mix, ffn2_norm, ffn2_w_in, ffn2_w_out, final_norm, p_2,
    positions_2, w_in_a_2, w_o_a_2, w_kv_b_2, w_in_b_2, w_o_b_2, ln_g_2, ln_b_2, w_ple_2,
    w_ple_gate_2,
):
    x = first_block(
        x, ffn1_norm, ffn1_w_in, ffn1_w_out, mix_norm, w_in_mix, w_pool, pool_scale, w_alpha,
        b_alpha, gla_norm, w_out_mix, ffn2_norm, ffn2_w_in, ffn2_w_out, final_norm,
    )
    return second_block(
        x, p_2, positions_2, w_in_a_2, w_o_a_2, w_kv_b_2, w_in_b_2, w_o_b_2, ln_g_2, ln_b_2,
        w_ple_2, w_ple_gate_2,
    )


_drawn_inputs = setup_inputs


def setup_inputs(seed=0):
    import zlib

    import numpy as np

    out = dict(_drawn_inputs(seed))
    spreads = {}
    factors = {'ffn1_norm': 6.188,
     'mix_norm': 3.862,
     'b_alpha': 8.0,
     'gla_norm': 8.0,
     'ffn2_norm': 8.0,
     'final_norm': 3.204}
    for name, (base, spread) in spreads.items():
        noise = np.random.default_rng([zlib.crc32(name.encode()), seed]).standard_normal(out[name].shape)
        drawn = base * np.exp(spread * noise) if base else spread * noise
        out[name] = __import__('jax').numpy.asarray(drawn.astype(out[name].dtype))
    for name, factor in factors.items():
        out[name] = (out[name] * factor).astype(out[name].dtype)
    return out
```

```python
from contextlib import ExitStack

import numpy as np

import concourse.bass as bass
from concourse import mybir

F32 = mybir.dt.float32
F32R = mybir.dt.float32r
I32 = mybir.dt.int32
ALU = mybir.AluOpType
ACT = mybir.ActivationFunctionType
AX = mybir.AxisListType

P = 128
SEQ = 256
TT = SEQ // P
D = 2048
KT = D // P
FF = 5632
NB = 512
HB = NB // 2
CH = 8
SPLIT = 4
EPS = 1e-6
LN_EPS = 1e-5
ALPHA = 4.0 ** 0.25
POOLS = (2, 4, 8, 16)
GH, GDK, GDV, CHUNK = 4, 128, 256, 64
HEADS, KVH, HD = 16, 4, 128
IH, ID = 16, 64
NSEL = 64
ROT, IROT = 16, 8
FAR = -3.0e38
TAKEN = -3.4e38
MAGIC = 1.5 * 2.0 ** 23
PI = 3.14159265
TWO_PI = (6.28125, 1.9350051879882812e-3, 3.0198e-7)
GAINS = 74
NORMED = ["ffn1_in0", "mix_pool", "ffn2_in0", "a_index"]
CONST = dict(ident=0, tri16=1, suf16=2, causal=3, strict=4, ntri=5, nones=6)


def shape_constants():
    i, j = np.arange(P)[:, None], np.arange(P)[None, :]
    same = (i // CHUNK) == (j // CHUNK)
    mats = [
        i == j,
        (same & (i <= j)) / 16.0,
        (same & (i > j)) / 16.0,
        same & (i <= j),
        i < j,
        -1.0 * (i > j),
        -np.ones((P, P)),
    ]
    inv_q = 1.0 / (500000.0 ** (np.arange(ROT) / ROT))
    inv_i = 1.0 / (500000.0 ** (np.arange(IROT) / IROT))
    rows = np.broadcast_to(np.concatenate([inv_q, inv_i]), (P, ROT + IROT))
    consts = np.concatenate([np.asarray(m, np.float32) for m in mats] + [rows], axis=1)
    s, t = np.arange(SEQ)[:, None], np.arange(SEQ)[None, :]
    band = [((t - s >= 0) & (t - s < w)) / np.minimum(t + 1, w) - (s == t) for w in POOLS]
    band = np.stack(band).reshape(len(POOLS), TT, P, SEQ).transpose(2, 0, 1, 3)
    return np.ascontiguousarray(consts, np.float32), np.ascontiguousarray(band, np.float32)


class Stage:

    def __init__(self, name, kind, n, tiles, pair, weights, width=NB):
        self.name, self.kind, self.n, self.tiles = name, kind, n, tiles
        self.pair, self.weights, self.width = pair, weights, width
        self.r0 = self.a0 = 0
        self.before = {}
        self.ahead = []
        self.early = []
        self.need = {}

    def chunk_tiles(self, c):
        if self.kind == "ple":
            return [c % 2]
        if self.tiles == KT:
            return [2 * c, 2 * c + 1]
        return [2 * c, 2 * c + 1] if c < 4 else [4 + c]


class Batch:

    def __init__(self, source, pair, kt, gain=None):
        self.source, self.pair, self.kt, self.gain = source, pair, kt, gain
        self.number = None


def paired_rounds(eng, stage, body):
    first = min(stage.n, 2) if stage.n > 4 else stage.n
    for k in range(first):
        body(k, k)
    if stage.n > first:
        with eng.Fori(0, (stage.n - first) // 2) as i:
            for u in range(2):
                body(i * 2 + (first + u), u)


def build(nc, A, out, upto=None):
    ctx = ExitStack()
    with ctx:
        def sb(name, shape, dt=F32):
            return ctx.enter_context(nc.sbuf_tensor(name, shape, dt))

        def overlaid(*groups):
            made = {}
            longest = max(groups, key=lambda g: sum(int(np.prod(s[1:])) for _, s, _ in g))
            for g in groups:
                if g is longest:
                    continue
                with ExitStack() as local:
                    for n, s, dt in g:
                        made[n] = local.enter_context(nc.sbuf_tensor(n, s, dt))
            for n, s, dt in longest:
                made[n] = sb(n, s, dt)
            return made

        sems = {}

        def sem(name):
            if name not in sems:
                sems[name] = ctx.enter_context(nc.semaphore(name))
            return sems[name]

        raw = sb("raw", [P, CH, 2, NB])
        whi = sb("whi", [P, SPLIT, 2, NB], F32R)
        wlo = sb("wlo", [P, SPLIT, 2, NB], F32R)
        ap = overlaid([("p_hi", [P, KT, SEQ], F32R), ("p_lo", [P, KT, SEQ], F32R)],
                      [("a_proj", [P, TT, 4096], F32)])
        aq = overlaid([("q_hi", [P, KT, SEQ], F32R), ("q_lo", [P, KT, SEQ], F32R)],
                      [("u", [P, TT, 3072], F32), ("pool_out", [P, 8, SEQ], F32)],
                      [("b_proj", [P, TT, 3072], F32), ("unit_q", [P, 4, NB], F32)])
        pair_hi = dict(P=ap["p_hi"], Q=aq["q_hi"])
        pair_lo = dict(P=ap["p_lo"], Q=aq["q_lo"])
        h = sb("h", [P, TT, D])
        at = overlaid([("tm", [P, TT, D], F32)], [("hid", [P, 2, TT, HB], F32)])
        tm, hid = at["tm"], at["hid"]
        ab = overlaid([("bc", [P, 2, D], F32)],
                      [("pooled", [P, 2, 2, SEQ], F32), ("walpha", [P, NB], F32),
                       ("balpha", [P, NB], F32), ("rt", [P, SEQ], F32), ("rtm", [P, TT, 16], F32)],
                      [("prob0", [P, 4, P], F32), ("prob1", [P, 4, SEQ], F32), ("probt", [P, 3, NB], F32)])
        bc = ab["bc"]
        sg = sb("sg", [P, 2, TT, HB])
        sgw = sg[:, :, :, :].rearrange("p a t n -> p a (t n)")
        ae = overlaid([("band", [P, 4, TT, SEQ], F32), ("wpool", [P, 4, 2, SEQ], F32), ("ex", [P, TT, NB], F32)],
                      [("state", [P, 3, GH * GDV], F32), ("scm", [P, TT, NB], F32)],
                      [("index_tail", [P, TT, 80], F32), ("isc", [P, TT, SEQ], F32), ("iwork", [P, TT, SEQ], F32),
                       ("amask", [P, TT, SEQ], F32), ("ikd", [P, TT, P], F32), ("ikt", [P, SEQ], F32),
                       ("kt_a", [P, KVH, SEQ], F32), ("rope_a", [P, 4, 4 * ROT], F32), ("rope_b", [P, 4, IH * IROT], F32)],
                      [("unit_e", [P, 5, NB], F32), ("unit_pad", [P, 1536], F32), ("ptm", [P, TT, SEQ], F32)],
                      [("pt_hi_pad", [P, TT, 1280], F32), ("pt_hi", [P, 2, SEQ], F32R),
                       ("pt_lo", [P, 2, SEQ], F32R)])
        pair_hi["E"], pair_lo["E"] = ae["pt_hi"], ae["pt_lo"]
        con = sb("con", [P, 7 * P + ROT + IROT])
        vrow = sb("vrow", [P, P])
        vec = sb("vec", [P, P])
        posi = sb("posi", [P, TT], I32)
        trig = sb("trig", [P, 6, TT, ROT + IROT])
        small = sb("small", [P, 96])
        bn = sb("bn", [P, TT, 4, 6])
        rsum = sb("rsum", [P, 8, 4])

        def const(name):
            return con[:, CONST[name] * P:(CONST[name] + 1) * P]

        ident = const("ident")
        parts = small[:, 0:8].rearrange("p (t n) -> p t n", t=TT)
        ssq, std, rstd = small[:, 8:10], small[:, 10:12], small[:, 12:14]
        eps_c, lneps_c, one_c = small[:, 14:15], small[:, 15:16], small[:, 16:17]
        mv = small[:, 18:22].rearrange("p (t n) -> p t n", t=TT)
        oss, ostd, orstd = small[:, 24:32], small[:, 32:40], small[:, 40:48]
        top8 = small[:, 48:56]
        nmax = small[:, 56:72].rearrange("p (b n) -> p b n", b=4)

        bank = [ctx.enter_context(nc.psum_tensor(f"bank{b}", [P, NB], F32)) for b in range(8)]
        MB = [6, 7, 4, 5]

        def ffn(tag, w_in, w_out, xs, hs):
            w3 = w_in.rearrange("k (s f) -> k s f", s=2)
            got, f0 = [], 0
            for g, n in enumerate((8, 8, 6)):
                got.append(Stage(f"{tag}_in{g}", "ffn_in", n, KT, xs, (w3, 0, f0)))
                got.append(Stage(f"{tag}_out{g}", "ffn_out", 4, 2 * n, hs, (w_out, f0, 0)))
                f0 += n * HB
            return got

        W = A
        stages = ffn("ffn1", W["ffn1_w_in"], W["ffn1_w_out"], "P", "Q")
        M, A1, B1 = W["w_in_mix"], W["w_in_a_2"], W["w_in_b_2"]
        stages += [Stage("mix_pool", "project", 2, KT, "P", (M, 0, 0)),
                   Stage("mix_decay", "project", 1, KT, "P", (M, 0, 4096), 16),
                   Stage("mix_qk", "project", 2, KT, "P", (M, 0, 1024)),
                   Stage("mix_v", "project", 2, KT, "P", (M, 0, 2048)),
                   Stage("mix_gate", "project", 2, KT, "P", (M, 0, 3072)),
                   Stage("mix_out", "mix_out", 4, KT, "P", (W["w_out_mix"], 0, 0))]
        stages += ffn("ffn2", W["ffn2_w_in"], W["ffn2_w_out"], "Q", "P")
        stages += [Stage("a_index", "project", 2, KT, "Q", (A1, 0, 5120)),
                   Stage("a_tail", "project", 1, KT, "Q", (A1, 0, 6144), 80),
                   Stage("a_kv", "project", 2, KT, "Q", (A1, 0, 2048)),
                   Stage("a_q", "project", 4, KT, "Q", (A1, 0, 0)),
                   Stage("a_gate", "head_gate", 4, KT, "Q", (A1, 0, 3072)),
                   Stage("a_out", "ln_out", 4, KT, "P", (W["w_o_a_2"], 0, 0)),
                   Stage("ple0", "ple", 1, 2, "E", (W["w_ple_2"][0], 0, 0)),
                   Stage("gate0", "gate", 4, KT, "Q", (W["w_ple_gate_2"][0], 0, 0)),
                   Stage("b_kv", "project", 2, KT, "P", (W["w_kv_b_2"], 0, 0)),
                   Stage("b_q", "project", 4, KT, "P", (B1, 0, 0)),
                   Stage("b_gate", "head_gate", 4, KT, "P", (B1, 0, 2048)),
                   Stage("b_out", "ln_out", 4, KT, "Q", (W["w_o_b_2"], 0, 0)),
                   Stage("ple1", "ple", 1, 2, "E", (W["w_ple_2"][1], 0, 0)),
                   Stage("gate1", "gate", 4, KT, "P", (W["w_ple_gate_2"][1], 0, 0))]
        if upto is not None:
            stages = stages[:[s.name for s in stages].index(upto) + 1]
        by_name = {s.name: s for s in stages}
        r = a = 0
        for s in stages:
            s.r0, s.a0 = r, a
            r, a = r + s.n, a + (4 if s.kind == "ple" else s.n)
        last = stages[-1]

        GAIN = dict(ffn1=0, mix=16, ffn2=32, final=48, pool=64, gla=72)

        def columns(buf, kt0=0):
            return lambda kt: [buf[:, t, (kt - kt0 + j) * P:(kt - kt0 + j + 1) * P] for j in range(2) for t in range(TT)]

        follows = {"ffn1_out2": ("P", "mix"), "mix_out": ("Q", "ffn2"), "ffn2_out2": ("Q", "final"), "gate0": ("P", None)}
        for n, s in enumerate(stages):
            nxt = stages[n + 1] if n + 1 < len(stages) else None
            if n == 0:
                s.ahead = [Batch(columns(h), "P", kt, GAIN["ffn1"]) for kt in range(0, KT, 2)]
            if s.name == "mix_out":
                s.before.setdefault(0, []).extend(Batch(columns(tm, 8), "P", kt, "gla") for kt in range(8, KT, 2))
            if s.kind == "ln_out":
                s.before.setdefault(1, []).append(Batch(columns(ae["ptm"]), "E", 0))
            if s.kind == "head_gate" and nxt:
                for k, blocks in ((2, (0, 1)), (3, (2,)), (4, (3,))):
                    where = s.before if k < s.n else nxt.before
                    where.setdefault(k % s.n, []).extend(
                        Batch(columns(tm), nxt.pair, 4 * blk + 2 * j) for blk in blocks for j in range(2))
            if s.kind == "gate":
                made = [Batch(columns(h), s.pair, kt) for kt in range(0, KT, 2)]
                s.ahead, s.early = made[0:4], made[4:6]
                s.before.setdefault(0, []).extend(made[6:8])
            if s.kind == "ffn_in" and nxt:
                s.hid_pair = nxt.pair
                nxt.before.setdefault(0, []).append(Batch(((s.n - 1) % 2,), nxt.pair, 2 * (s.n - 1)))
            if s.name in follows and nxt:
                pair, gain = follows[s.name]
                for k in range(s.n):
                    where = s.before if k + 1 < s.n else nxt.before
                    where.setdefault((k + 1) % s.n, []).extend(
                        Batch(columns(h), pair, 4 * k + 2 * j, GAIN[gain] if gain else None) for j in range(2))
        n, latest = 0, {}
        for s in stages:
            for b in s.ahead:
                b.number, latest[b.pair, b.kt], n = n, n, n + 1
            for k in range(s.n):
                for c in range(CH):
                    if c == 2 and k == 0:
                        for b in s.early:
                            b.number, latest[b.pair, b.kt], n = n, n, n + 1
                    if c == 4:
                        for b in s.before.get(k, []):
                            b.number, latest[b.pair, b.kt], n = n, n, n + 1
                        if s.kind == "ffn_in" and k:
                            if k == 1:
                                s.hid_batch0 = n
                            latest[s.hid_pair, 2 * (k - 1)], n = n, n + 1
                    if k == 0:
                        s.need[c] = latest[s.pair, s.chunk_tiles(c)[-1] // 2 * 2] + 1

        def batches_of(s, k, peeled):
            got = list(s.before.get(k, [])) if peeled else []
            if s.kind == "ffn_in" and not (peeled and k == 0):
                got.append(("hid", k))
            return got

        def resolve(s, b, u):
            if isinstance(b, Batch):
                return b.number, b.number % 2, b.pair, b.kt, b.gain
            k = b[1]
            return k - 1 + s.hid_batch0, (u - 1 + s.hid_batch0) % 2, s.hid_pair, (k - 1) * 2, None

        def acc(a, t):
            return bank[(a % 2) * 2 + t]

        def acc_par(s, u, t):
            return bank[((s.a0 + u) % 2) * 2 + t]

        uses, count = {}, {b: 0 for b in range(8)}

        def plan(name, m):
            b = MB[m]
            uses[name] = (b, count[b])
            count[b] += 1

        plan("vec", 0)
        if "mix_qk" in by_name:
            for name, m in (("sum0", 0), ("sum1", 1), ("y0", 2), ("sum2", 0), ("y1", 3), ("sum3", 1), ("y2", 2), ("y3", 3),
                            ("rT", 0), ("z0", 0), ("z1", 1), ("b0", 0), ("suf0", 2), ("b1", 1), ("suf1", 3),
                            ("qT0", 0), ("kT0", 2), ("qT1", 1), ("kT1", 3), ("sc0", 0), ("sc1", 1),
                            ("kv00", 2), ("kv01", 3), ("kv10", 0), ("kv11", 1), ("kv20", 2), ("kv21", 3),
                            ("og00", 0), ("og01", 1), ("og10", 2), ("og11", 3)):
                plan(name, m)
        if "a_kv" in by_name:
            for n, name in enumerate(("ik", "iq00", "iq01", "iq10", "iq11")):
                plan(name, n % 4)
            for n in range(16):
                plan(f"x{n}", n % 4)
            for t in range(TT):
                plan(f"ka{t}", t)
            for g in range(KVH):
                for name, m in (("qa0", 0), ("qa1", 1), ("l0", 2), ("l10", 3), ("l11", 0), ("pt0", 1), ("pt10", 2), ("pt11", 3),
                                ("oa0", 0), ("oa1", 1)):
                    plan(f"{name}_{g}", m)
        if "b_kv" in by_name:
            for t in range(TT):
                plan(f"kb{t}", t)
            for g in range(KVH):
                for name, m in (("qb0", 0), ("qb1", 1), ("zb0", 2), ("zb1", 3), ("zb2", 0), ("fb0", 1), ("fb1", 2), ("fb2", 3),
                                ("ob0", 0), ("ob1", 1)):
                    plan(f"{name}_{g}", m)

        full = [sem(f"bank_full_{b}") for b in range(8)]
        freed_s = [sem(f"bank_freed_{b}") for b in range(8)]

        emitted = {b: 0 for b in range(8)}
        issued = [0]

        def use(name):
            b, n = uses[name]
            assert emitted[b] == n, name
            emitted[b] += 1
            if n:
                nc.tensor.wait_ge(freed_s[b], n)
            if b in (4, 5) and issued[0]:
                nc.tensor.wait_ge(t_done, issued[0])
            return bank[b]

        def filled(ins, name):
            ins.then_inc(full[uses[name][0]], 1)

        def take(eng, name):
            b, n = uses[name]
            eng.wait_ge(full[b], n + 1)
            return bank[b]

        def release(ins, name):
            ins.then_inc(freed_s[uses[name][0]], 1)

        def wait_freed(eng, name):
            b, n = uses[name]
            eng.wait_ge(freed_s[b], n + 1)

        landed = [sem(f"weights_landed_{c}") for c in range(CH)]
        hi_done, lo_done, chunk_used = sem("weights_hi_done"), sem("weights_lo_done"), sem("chunk_used")
        acc_free = sem("acc_free")
        t_full, t_hi, t_done = sem("transposed"), sem("operand_hi_done"), sem("operand_done")
        silu_done = sem("silu_done")
        const_in, x_in = sem("const_in"), sem("x_in")
        side_in = sem("side_in")

        LO0, USED0, FREE0 = CH, SPLIT, 2


        def width_of(s, k):
            return stages[stages.index(s) + 1].width if isinstance(k, int) and k == s.n else s.width

        def sums_done(eng, s, k):
            eng.wait_ge(chunk_used, (s.r0 + k) * CH + (CH + USED0))

        def attention_done(eng, stage):
            for t in range(TT):
                wait_freed(eng, f"{'oa' if stage == 'a_out' else 'ob'}{t}_{KVH - 1}")

        def angles(dve, link):
            posf = small[:, 72:74]
            dve.wait_ge(sem("pos_in"), 16)
            dve.wait_ge(const_in, 16)
            link(dve.tensor_copy(posf, posi[:, :]))
            ang, turns, left = (trig[:, i, :, :] for i in range(3))
            for t in range(TT):
                ins = dve.tensor_scalar(trig[:, 0, t, :], con[:, 7 * P:7 * P + ROT + IROT], posf[:, t:t + 1], None, ALU.mult)
            link(ins)
            link(dve.tensor_scalar(turns, ang, 1.0 / (2.0 * np.pi), MAGIC, ALU.mult, ALU.add))
            link(dve.tensor_scalar(turns, turns, MAGIC, None, ALU.subtract))
            link(dve.scalar_tensor_tensor(left, turns, -TWO_PI[0], ang, ALU.mult, ALU.add))
            for part in TWO_PI[1:]:
                link(dve.scalar_tensor_tensor(left, turns, -part, left, ALU.mult, ALU.add))
            dve.tensor_scalar(left, left, PI, -PI, ALU.min, ALU.max).then_inc(sem("trig_args"), 1)

        UQ, UK, UV = 1024, 1536, 2048

        def cols(t, first, n=P):
            return aq["u"][:, t, first:first + n]

        def gla_pe(pe, stage, k, c):
            u, pooled, band, wpool = aq["u"], ab["pooled"], ae["band"], ae["wpool"]
            la, kinv = tm[:, :, 1024:1536], tm[:, :, 1536:2048]

            def pool_sums(g):
                b = use(f"sum{g}")
                for j in range(2):
                    x = (2 * g + j) * P
                    pe.matmul(b[:, j * SEQ:(j + 1) * SEQ], u[:, 0, x:x + P], band[:, g, 0, :], start=True, stop=False)
                    ins = pe.matmul(b[:, j * SEQ + P:(j + 1) * SEQ], u[:, 1, x:x + P], band[:, g, 1, P:SEQ], start=False, stop=True)
                filled(ins, f"sum{g}")

            def pool_maps(g):
                wait_freed(pe, f"sum{g}")
                b = use(f"y{g}")
                for j in range(2):
                    for i in range(2):
                        ins = pe.matmul(b[:, j * SEQ:(j + 1) * SEQ], wpool[:, g, i, j * P:(j + 1) * P],
                                        pooled[:, g % 2, i, :], start=(i == 0), stop=(i == 1))
                filled(ins, f"y{g}")

            def chunk_states(n):
                t, half = n // 2, n % 2
                rows = slice(half * CHUNK, (half + 1) * CHUNK)
                pe.wait_ge(sem("ktail_done"), t + 1)
                for j in range(2):
                    b = use(f"kv{n}{j}")
                    for hd in (2 * j, 2 * j + 1):
                        ins = pe.matmul(b[:, (hd % 2) * GDV:(hd % 2 + 1) * GDV], u[rows, t, UK + hd * P:UK + (hd + 1) * P],
                                        u[rows, t, UV + hd * GDV:UV + (hd + 1) * GDV], start=True, stop=True)
                    filled(ins, f"kv{n}{j}")

            def outputs(t):
                for j in range(2):
                    b = use(f"og{t}{j}")
                    for n in ((0,), (1, 2))[t]:
                        wait_freed(pe, f"kv{n}{j}")
                    for hd in (2 * j, 2 * j + 1):
                        o = slice((hd % 2) * GDV, (hd % 2 + 1) * GDV)
                        ins = pe.matmul(b[:, o], ae["scm"][:, t, hd * P:(hd + 1) * P], cols(t, UV + hd * GDV, GDV), start=True, stop=False,
                                        skip_group_check=True)
                        for half in range(2):
                            n = 2 * t + half
                            if n:
                                ins = pe.matmul(b[half * CHUNK:(half + 1) * CHUNK, o], cols(t, UQ + hd * P + half * CHUNK, CHUNK),
                                                ae["state"][:, n - 1, hd * GDV:(hd + 1) * GDV], start=False, stop=True,
                                                skip_group_check=True)
                    filled(ins, f"og{t}{j}")

            step = (stage, k, c)
            if step == ("mix_qk", 0, 0):
                pe.wait_ge(sem("pool_in"), 64)
                pe.wait_ge(sem("ones_done"), 1)
                pe.wait_ge(acc_free, by_name["mix_decay"].a0 + 1 + FREE0)
                pool_sums(0)
            elif stage == "mix_qk" and k == 0 and c in (1, 2, 3):
                pool_sums(c)
                pool_maps(c - 1)
            elif step == ("mix_qk", 0, 4):
                pool_maps(3)
                b = use("rT")
                for t in range(TT):
                    ins = pe.transpose(b[0:16, t * P:(t + 1) * P], ab["rtm"][:, t, :], ident)
                filled(ins, "rT")
            elif step == ("mix_qk", 0, 5):
                wait_freed(pe, "rT")
                for t in range(TT):
                    b = use(f"z{t}")
                    pe.matmul(b[:, :], ab["rt"][0:16, t * P:(t + 1) * P], ab["walpha"][0:16, :], start=True, stop=False)
                    filled(pe.matmul(b[:, :], vrow[0:1, :], ab["balpha"][0:1, :], start=False, stop=True), f"z{t}")
            elif step == ("mix_qk", 1, 1):
                for t in range(TT):
                    wait_freed(pe, f"z{t}")
                    b = use(f"b{t}")
                    for hd in range(GH):
                        ins = pe.matmul(b[:, hd * P:(hd + 1) * P], la[:, t, hd * P:(hd + 1) * P], const("tri16"), start=True, stop=True)
                    filled(ins, f"b{t}")
                    filled(pe.matmul(use(f"suf{t}")[:, :], const("suf16"), la[:, t, :], start=True, stop=True), f"suf{t}")
            elif step == ("mix_v", 0, 1):
                pe.wait_ge(acc_free, by_name["mix_qk"].a0 + 2 + FREE0)
                for t in range(TT):
                    for name, first in (("qT", UQ), ("kT", UK)):
                        b = use(f"{name}{t}")
                        for hd in range(GH):
                            ins = pe.transpose(b[:, hd * P:(hd + 1) * P], cols(t, first + hd * P), ident)
                        filled(ins, f"{name}{t}")
            elif step == ("mix_v", 0, 5):
                for t in range(TT):
                    wait_freed(pe, f"qT{t}")
                    wait_freed(pe, f"kT{t}")
                    b = use(f"sc{t}")
                    for hd in range(GH):
                        ins = pe.matmul(b[:, hd * P:(hd + 1) * P], kinv[:, t, hd * P:(hd + 1) * P], cols(t, UQ + hd * P), start=True, stop=True)
                    filled(ins, f"sc{t}")
            elif step == ("mix_gate", 0, 1):
                pe.wait_ge(acc_free, by_name["mix_v"].a0 + 2 + FREE0)
                chunk_states(0)
            elif step == ("mix_gate", 0, 2):
                wait_freed(pe, "sc0")
                wait_freed(pe, "sc1")
                chunk_states(1)
            elif step == ("mix_gate", 0, 4):
                chunk_states(2)
            elif step == ("mix_gate", 0, 6):
                outputs(0)
            elif step == ("mix_gate", 0, 7):
                outputs(1)

        def gla_act(act, stage, k, c):
            pooled, ex, soft = ab["pooled"], ae["ex"], tm[:, :, 1536:2048]
            up, down = aq["u"][:, :, 0:512], aq["u"][:, :, 512:1024]
            step = (stage, k, c)
            if stage == "mix_qk" and k == 0 and c < 4:
                release(act.copy(pooled[:, c % 2, :, :], take(act, f"sum{c}")[:, :].rearrange("p (i n) -> p i n", i=2)), f"sum{c}")
            elif step == ("mix_qk", 0, 4):
                release(act.copy(ab["rt"][0:16, :], take(act, "rT")[0:16, 0:SEQ]), "rT")
            elif step == ("mix_qk", 0, 5):
                act.preload_act_table_set("natural_log_exp_and_others")
                n = 0
                for t in range(TT):
                    b = take(act, f"z{t}")
                    for src, func, scale, bias, dst in ((b[:, :], ACT.Abs, 1.0, 0.0, ex[:, t, :]), (ex[:, t, :], ACT.Exp, -1.0, 0.0, ex[:, t, :]),
                                                        (ex[:, t, :], ACT.Ln, 1.0, 1.0, soft[:, t, :])):
                        if n:
                            act.wait_ge(sem("softplus_step"), n)
                        act.activation(dst, src, func, scale=scale, bias=bias).then_inc(sem("softplus_step"), 1)
                        n += 1
            elif step == ("mix_qk", 1, 1):
                for t in range(TT):
                    b = take(act, f"b{t}")
                    act.activation(up[:, t, :], b[:, :], ACT.Exp)
                    release(act.activation(down[:, t, :], b[:, :], ACT.Exp, scale=-1.0), f"b{t}")
                    release(act.activation(ex[:, t, :], take(act, f"suf{t}")[:, :], ACT.Exp), f"suf{t}")
            elif step == ("mix_gate", 0, 7):
                act.wait_ge(sem("ktail_done"), 2)
                for t in range(TT):
                    for j in range(2):
                        b = take(act, f"og{t}{j}")
                        for i in range(2):
                            hd = 2 * j + i
                            sink = (ex, down)[t][:, j, i * GDV:(i + 1) * GDV]
                            ins = act.activation(sink, b[:, i * GDV:(i + 1) * GDV], ACT.Square,
                                                 accum_out=oss[:, t * 4 + hd:t * 4 + hd + 1])
                ins.then_inc(sem("head_squares"), 1)
                act.wait_ge(sem("head_squares"), 1)
                act.activation(ostd, oss, ACT.Sqrt, bias=eps_c, scale=1.0 / GDV).then_inc(sem("head_root"), 1)

        def gla_heads_out(dve, j):
            dve.wait_ge(acc_free, by_name["mix_gate"].a0 + j + 1 + FREE0)
            for t in range(TT):
                b = take(dve, f"og{t}{j}")
                for i in range(2):
                    hd = 2 * j + i
                    v_ = slice(hd * GDV, (hd + 1) * GDV)
                    ins = dve.scalar_tensor_tensor(tm[:, t, v_], b[:, i * GDV:(i + 1) * GDV], orstd[:, t * 4 + hd:t * 4 + hd + 1],
                                                   tm[:, t, 1024 + hd * GDV:1024 + (hd + 1) * GDV], ALU.mult, ALU.mult)
                release(ins, f"og{t}{j}")

        def gla_dve(dve, link, stage, k, c):
            scm, ex, state = ae["scm"], ae["ex"], ae["state"]
            up, down = aq["u"][:, :, 0:512], aq["u"][:, :, 512:1024]
            la, soft = tm[:, :, 1024:1536], tm[:, :, 1536:2048]
            step = (stage, k, c)
            if stage == "mix_qk" and k == 0 and 1 <= c <= 4:
                g = c - 1
                b = take(dve, f"y{g}")
                for j in range(2):
                    s_ = GAIN["pool"] + 2 * g + j
                    ins = dve.tensor_scalar(aq["pool_out"][:, 2 * g + j, :], b[:, j * SEQ:(j + 1) * SEQ], vec[:, s_:s_ + 1], None, ALU.mult)
                release(ins, f"y{g}")
            elif step == ("mix_qk", 0, 7):
                for t in range(TT):
                    dve.wait_ge(sem("softplus_step"), 3 * (t + 1))
                    release(dve.scalar_tensor_tensor(la[:, t, :], take(dve, f"z{t}")[:, :], 0.0, soft[:, t, :], ALU.min, ALU.subtract), f"z{t}")
            elif step == ("mix_qk", 1, 4):
                dve.memset(scm[:, :, :], 0.0).then_inc(sem("scores_cleared"), 1)
            elif stage == "mix_v" and k == 0 and c in (1, 2):
                t = c - 1
                wait_freed(dve, f"b{t}")
                release(dve.scalar_tensor_tensor(cols(t, UQ, NB), take(dve, f"qT{t}")[:, :], float(GDK) ** -0.5, up[:, t, :], ALU.mult, ALU.mult), f"qT{t}")
                release(dve.tensor_tensor(soft[:, t, :], take(dve, f"kT{t}")[:, :], down[:, t, :], ALU.mult), f"kT{t}")
                wait_freed(dve, f"suf{t}")
                dve.tensor_tensor(cols(t, UK, NB), cols(t, UK, NB), ex[:, t, :], ALU.mult).then_inc(sem("ktail_done"), 1)
            elif step == ("mix_v", 0, 5):
                dve.wait_ge(sem("scores_cleared"), 1)
                mask = const("causal").unsqueeze(1).to_broadcast([P, GH, P]).bitcast(I32)
                for t in range(TT):
                    release(dve.copy_predicated(scm[:, t, :].rearrange("p (a b) -> p a b", a=GH), mask,
                                                take(dve, f"sc{t}")[:, :].rearrange("p (a b) -> p a b", a=GH)), f"sc{t}")
            elif stage == "mix_gate" and k == 0 and c in (1, 2, 4):
                n = (1, 2, 4).index(c)
                for j in range(2):
                    b = take(dve, f"kv{n}{j}")
                    if n == 0:
                        ins = dve.tensor_copy(state[:, 0, j * NB:(j + 1) * NB], b[:, :])
                    else:
                        wait_freed(dve, f"kv{n - 1}{j}")
                        t, half = n // 2, n % 2
                        for hd in (2 * j, 2 * j + 1):
                            end = hd * P + half * CHUNK + CHUNK - 1
                            v_ = slice(hd * GDV, (hd + 1) * GDV)
                            ins = dve.scalar_tensor_tensor(state[:, n, v_], state[:, n - 1, v_], up[:, t, end:end + 1],
                                                           b[:, (hd % 2) * GDV:(hd % 2 + 1) * GDV], ALU.mult, ALU.add)
                    release(ins, f"kv{n}{j}")
            elif step == ("mix_gate", 1, 1):
                dve.wait_ge(sem("head_root"), 1)
                link(dve.reciprocal(orstd, ostd))
                gla_heads_out(dve, 0)

        AK, AV, AI = 2048, 2560, 3072

        def group_of(first, gate, stage, k):
            if stage == first and k:
                return k - 1
            return KVH - 1 if stage == gate and k == 0 else None

        def index_use(n):
            return n // 8, n % 8 // 2 * 2, n % 2

        def index_step(stage, k, c):
            i = k * CH + c - 4 if stage == "a_kv" else -1
            return range(2 * i, 2 * i + 2) if 0 <= i < 8 else ()

        def attention_a_pe(pe, stage, k, c):
            proj, kt_, ikt = ap["a_proj"], ae["kt_a"], ae["ikt"]
            g = group_of("a_q", "a_gate", stage, k)
            step = (stage, k, c)
            if step == ("a_kv", 0, 2):
                pe.wait_ge(sem("index_rotated"), 1)
                b = use("ik")
                for t in range(TT):
                    ins = pe.transpose(b[:, t * P:(t + 1) * P], ae["ikd"][:, t, :], ident)
                filled(ins, "ik")
            if stage == "a_kv" and k == 0 and c in (2, 3):
                for name in (("iq00", "iq01", "iq10"), ("iq11",))[c - 2]:
                    t, j = int(name[2]), int(name[3])
                    b = use(name)
                    for i in range(4):
                        x = AI + (4 * j + i) * P
                        ins = pe.transpose(b[:, i * P:(i + 1) * P], proj[:, t, x:x + P], ident)
                    filled(ins, name)
            for n in index_step(stage, k, c):
                t, pair0, half = index_use(n)
                S = P * (t + 1)
                if n == 0:
                    wait_freed(pe, "ik")
                wait_freed(pe, f"iq{t}{pair0 // 4}")
                b = use(f"x{n}")
                rows = slice(half * ID, (half + 1) * ID)
                for i in range(2):
                    x = AI + (pair0 + i) * P
                    ins = pe.matmul(b[:, i * S:(i + 1) * S], proj[rows, t, x:x + P], ikt[rows, 0:S], start=True, stop=True)
                filled(ins, f"x{n}")
            if step == ("a_q", 0, 2):
                pe.wait_ge(sem("head_rotation_step"), 2 * TT)
                for t in range(TT):
                    b = use(f"ka{t}")
                    for i in range(4):
                        ins = pe.transpose(b[:, i * P:(i + 1) * P], proj[:, t, AK + i * P:AK + (i + 1) * P], ident)
                    filled(ins, f"ka{t}")
            if g is None:
                return
            if c == 1:
                pe.wait_ge(sem("head_rotation_step"), 2 * TT * (g + 2))
                for t in range(TT):
                    b = use(f"qa{t}_{g}")
                    for i in range(4):
                        ins = pe.transpose(b[:, i * P:(i + 1) * P], proj[:, t, g * NB + i * P:g * NB + (i + 1) * P], ident)
                    filled(ins, f"qa{t}_{g}")
            if c == 2:
                for t in range(TT):
                    wait_freed(pe, f"ka{t}")
                for t, name, i0, n in ((0, "l0", 0, 4), (1, "l10", 0, 2), (1, "l11", 2, 2)):
                    wait_freed(pe, f"qa{t}_{g}")
                    S = P * (t + 1)
                    b = use(f"{name}_{g}")
                    for i in range(n):
                        x = g * NB + (i0 + i) * P
                        ins = pe.matmul(b[:, i * S:(i + 1) * S], proj[:, t, x:x + P], kt_[:, g, 0:S], start=True, stop=True)
                    filled(ins, f"{name}_{g}")
            if c == 5:
                for t, name, st in ((0, "pt0", 0), (1, "pt10", 0), (1, "pt11", 1)):
                    pe.wait_ge(sem("exp_done"), 2 * g + t + 1)
                    b = use(f"{name}_{g}")
                    for i in range(4):
                        ins = pe.transpose(b[:, i * P:(i + 1) * P], ab[f"prob{t}"][:, i, st * P:(st + 1) * P], ident)
                    filled(ins, f"{name}_{g}")
            if c == 7:
                for t, names in ((0, ("pt0",)), (1, ("pt10", "pt11"))):
                    for name in names:
                        wait_freed(pe, f"{name}_{g}")
                    b = use(f"oa{t}_{g}")
                    for i in range(4):
                        for st in range(t + 1):
                            ins = pe.matmul(b[:, i * P:(i + 1) * P], ab["probt"][:, t + st, i * P:(i + 1) * P],
                                            proj[:, st, AV + g * P:AV + (g + 1) * P], start=(st == 0), stop=(st == t))
                    filled(ins, f"oa{t}_{g}")

        def attention_a_act(act, stage, k, c):
            proj = ap["a_proj"]
            g = group_of("a_q", "a_gate", stage, k)
            step = (stage, k, c)
            if step == ("a_kv", 0, 2):
                release(act.copy(ae["ikt"][:, :], take(act, "ik")[:, 0:SEQ]), "ik")
            if stage == "a_kv" and k == 0 and c in (2, 3):
                for name in (("iq00", "iq01", "iq10"), ("iq11",))[c - 2]:
                    t, j = int(name[2]), int(name[3])
                    release(act.copy(proj[:, t, AI + j * NB:AI + (j + 1) * NB], take(act, name)[:, :]), name)
            for n in index_step(stage, k, c):
                S = P * (n // 8 + 1)
                b = take(act, f"x{n}")
                if n >= 2:
                    act.wait_ge(sem("relu_used"), n - 1)
                release(act.activation(sgw[:, n % 2, 0:2 * S], b[:, 0:2 * S], ACT.Relu), f"x{n}")
            if step == ("a_q", 0, 2):
                for t in range(TT):
                    release(act.copy(ae["kt_a"][:, :, t * P:(t + 1) * P], take(act, f"ka{t}")[:, :].rearrange("p (a n) -> p a n", a=4)), f"ka{t}")
            if g is None:
                return
            if c == 1:
                for t in range(TT):
                    release(act.copy(proj[:, t, g * NB:(g + 1) * NB], take(act, f"qa{t}_{g}")[:, :]), f"qa{t}_{g}")
            if c in (2, 3):
                t = c - 2
                act.wait_ge(sem("max_done"), 2 * g + t + 1)
                for i in range(4):
                    pr = ab[f"prob{t}"][:, i, :]
                    ins = act.activation(pr, pr, ACT.Exp, bias=nmax[:, t, i:i + 1], accum_out=rsum[:, 2 * g + t, i:i + 1])
                ins.then_inc(sem("exp_done"), 1)
            if c == 5:
                for i, name in enumerate(("pt0", "pt10", "pt11")):
                    release(act.copy(ab["probt"][:, i, :], take(act, f"{name}_{g}")[:, :]), f"{name}_{g}")

        rotated = dict(head_rotation=0, index_rotation=0)

        def rotate(eng, view, heads, half, c0, tmp, tag):
            for t in range(TT):
                x1, x2 = view[t][:, :, 0:half], view[t][:, :, half:2 * half]
                cos = trig[:, 5, t, c0:c0 + half].unsqueeze(1).to_broadcast([P, heads, half])
                sin = trig[:, 3, t, c0:c0 + half].unsqueeze(1).to_broadcast([P, heads, half])
                part = [tmp[:, i, 0:heads * half].rearrange("p (a b) -> p a b", a=heads) for i in range(4)]
                for dst, x, f in zip(part, (x1, x2, x1, x2), (cos, sin, sin, cos)):
                    ins = eng.tensor_tensor(dst, x, f, ALU.mult)
                rotated[tag] += 1
                ins.then_inc(sem(f"{tag}_step"), 1)
                eng.wait_ge(sem(f"{tag}_step"), rotated[tag])
                eng.tensor_tensor(x1, part[0], part[1], ALU.subtract)
                rotated[tag] += 1
                eng.tensor_tensor(x2, part[2], part[3], ALU.add).then_inc(sem(f"{tag}_step"), 1)
                eng.wait_ge(sem(f"{tag}_step"), rotated[tag])

        def mixer_a_pool(pool):
            tail, proj = ae["index_tail"], ap["a_proj"]
            pool.wait_ge(acc_free, by_name["a_tail"].a0 + 1 + FREE0)
            pool.wait_ge(sem("cos_done"), 1)
            view = [tail[:, t, 0:ID].rearrange("p (a b) -> p a b", a=1) for t in range(TT)]
            rotate(pool, view, 1, IROT, ROT, ae["rope_b"], "index_rotation")
            view = [proj[:, t, AI:AI + IH * ID].rearrange("p (a b) -> p a b", a=IH) for t in range(TT)]
            rotate(pool, view, IH, IROT, ROT, ae["rope_b"], "index_rotation")
            for t in range(TT):
                for j in range(2):
                    ins = pool.tensor_copy(ae["ikd"][:, t, j * ID:(j + 1) * ID], tail[:, t, 0:ID])
            ins.then_inc(sem("index_rotated"), 1)
            for t in range(TT):
                pool.wait_ge(sem("relu_used"), 8 * (t + 1))
                diag = ae["isc"][:, t, t * P:(t + 1) * P]
                pool.affine_select(out=diag, in_=diag, pattern=[[-1, P]], compare_op=ALU.is_ge, fill=FAR, base=0,
                                   channel_multiplier=1).then_inc(sem("index_masked"), 1)

        def attention_a_dve(dve, link, stage, k, c):
            tail, isc, work, am, proj = ae["index_tail"], ae["isc"], ae["iwork"], ae["amask"], ap["a_proj"]
            g = group_of("a_q", "a_gate", stage, k)
            step = (stage, k, c)
            if step == ("a_index", 0, 0):
                dve.wait_ge(sem("trig_done"), 1)
                link(dve.tensor_tensor(trig[:, 5, :, :], trig[:, 4, :, :], trig[:, 4, :, :], ALU.mult))
                dve.tensor_scalar(trig[:, 5, :, :], trig[:, 5, :, :], -2.0, 1.0, ALU.mult, ALU.add).then_inc(sem("cos_done"), 1)
                dve.wait_ge(sem("cos_done"), 1)
            if step == ("a_kv", 0, 0):
                dve.wait_ge(acc_free, by_name["a_tail"].a0 + 1 + FREE0)
                iw = tail[:, :, ID:ID + IH]
                link(dve.tensor_scalar(iw, iw, float(ID) ** -0.5 * float(IH) ** -0.5, None, ALU.mult))
            if stage == "a_kv" and k == 0 and c in (0, 1):
                dve.wait_ge(sem("final_in"), 16)
                dve.scalar_tensor_tensor(h[:, c, :], h[:, c, :], rstd[:, c:c + 1], bc[:, 0, :], ALU.mult, ALU.mult).then_inc(sem("residual_done"), 1)
            for n in index_step(stage, k, c):
                t, pair0, half = index_use(n)
                S = P * (t + 1)
                wait_freed(dve, f"x{n}")
                for i in range(2):
                    hd = 2 * (pair0 + i) + half
                    rl, w_ = sgw[:, n % 2, i * S:(i + 1) * S], tail[:, t, ID + hd:ID + hd + 1]
                    if n % 8 == i == 0:
                        ins = dve.tensor_scalar(isc[:, t, 0:S], rl, w_, None, ALU.mult)
                    else:
                        ins = dve.scalar_tensor_tensor(isc[:, t, 0:S], rl, w_, isc[:, t, 0:S], ALU.mult, ALU.add)
                    if i == 0:
                        link(ins)
                ins.then_inc(sem("relu_used"), 1)
                dve.wait_ge(sem("relu_used"), n + 1)
            turns = {("a_kv", 1, 1): (0, range(0, 4)), ("a_kv", 1, 3): (0, range(4, 8)), ("a_kv", 1, 5): (1, range(0, 3)),
                     ("a_kv", 1, 6): (1, range(3, 6)), ("a_kv", 1, 7): (1, range(6, 8))}.get(step)
            if turns:
                t = turns[0]
                S = P * (t + 1)
                for n in turns[1]:
                    if n == 0:
                        dve.wait_ge(sem("index_masked"), t + 1)
                    src = work[:, t, 0:S] if n else isc[:, t, 0:S]
                    link(dve.max(top8, src))
                    link(dve.match_replace(work[:, t, 0:S], top8, src, TAKEN))
                if n == NSEL // 8 - 1:
                    link(dve.tensor_tensor(work[:, t, 0:S], work[:, t, 0:S], isc[:, t, 0:S], ALU.is_lt))
                    link(dve.scalar_tensor_tensor(work[:, t, 0:S], isc[:, t, 0:S], FAR * 0.5, work[:, t, 0:S], ALU.is_gt, ALU.mult))
                    link(dve.tensor_scalar(am[:, t, 0:S], work[:, t, 0:S], 1.0, 1.0e30, ALU.subtract, ALU.mult))
            if step == ("a_q", 0, 0):
                dve.wait_ge(acc_free, by_name["a_kv"].a0 + 2 + FREE0)
                view = [proj[:, t, AK:AK + NB].rearrange("p (a b) -> p a b", a=4) for t in range(TT)]
                rotate(dve, view, 4, ROT, 0, ae["rope_a"], "head_rotation")
            if g is None:
                return
            if c == 0:
                dve.wait_ge(acc_free, by_name["a_q"].a0 + g + 1 + FREE0)
                view = [proj[:, t, g * NB:(g + 1) * NB].rearrange("p (a b) -> p a b", a=4) for t in range(TT)]
                rotate(dve, view, 4, ROT, 0, ae["rope_a"], "head_rotation")
            if c in (2, 3):
                t = c - 2
                S, per = P * (t + 1), 4 // (t + 1)
                names = (("l0",), ("l10", "l11"))[t]
                if t == 0 and g == 0:
                    dve.wait_ge(sem("residual_done"), 2)
                for j, name in enumerate(names):
                    b = take(dve, f"{name}_{g}")
                    mask = am[:, t, 0:S].unsqueeze(1).to_broadcast([P, per, S])
                    ins = dve.scalar_tensor_tensor(ab[f"prob{t}"][:, j * per:(j + 1) * per, :],
                                                   b[:, 0:per * S].rearrange("p (a b) -> p a b", a=per), float(HD) ** -0.5, mask,
                                                   ALU.mult, ALU.add)
                    release(ins, f"{name}_{g}")
                wait_freed(dve, f"{names[-1]}_{g}")
                dve.tensor_reduce(nmax[:, t, :], ab[f"prob{t}"][:, :, :], AX.X, ALU.max, negate=True).then_inc(sem("max_done"), 1)
            if c == 7:
                for t in range(TT):
                    dve.wait_ge(sem("exp_done"), 2 * g + t + 1)
                    r_ = rsum[:, 2 * g + t, :]
                    link(dve.reciprocal(r_, r_))
                    b = take(dve, f"oa{t}_{g}")
                    release(dve.tensor_tensor(tm[:, t, g * NB:(g + 1) * NB].rearrange("p (a b) -> p a b", a=4),
                                              b[:, :].rearrange("p (a b) -> p a b", a=4),
                                              r_.unsqueeze(2).to_broadcast([P, 4, P]), ALU.mult), f"oa{t}_{g}")

        PAIRS = ((0, 0), (1, 0), (1, 1))
        BK, BV = 2048, 2560

        def unit(i):
            places = [aq["unit_q"][:, n, :] for n in range(4)] + [ae["unit_e"][:, n, :] for n in range(5)]
            return places[3 * i:3 * i + 3]

        def last_group(stage, k):
            if stage == "b_gate" and k < 2:
                return KVH - 2 + k
            return k - 2 if stage == "b_q" and k >= 2 else None

        def attention_b_pe(pe, stage, k, c):
            proj = aq["b_proj"]
            g, before = group_of("b_q", "b_gate", stage, k), last_group(stage, k)
            if (stage, k, c) == ("b_q", 0, 1):
                pe.wait_ge(acc_free, by_name["b_kv"].a0 + 2 + FREE0)
                for t in range(TT):
                    b = use(f"kb{t}")
                    for i in range(4):
                        ins = pe.transpose(b[:, i * P:(i + 1) * P], proj[:, t, BK + i * P:BK + (i + 1) * P], ident)
                    filled(ins, f"kb{t}")
            if before is not None and c == 0:
                pe.wait_ge(sem("weights_masked"), 2 * before + 2)
                pe.wait_ge(sem("stick_exp"), 3 * before + 3)
                for t in range(TT):
                    b = use(f"ob{t}_{before}")
                    for i in range(4):
                        for st in range(t + 1):
                            ins = pe.matmul(b[:, i * P:(i + 1) * P], unit(t + st)[2][:, i * P:(i + 1) * P],
                                            proj[:, st, BV + before * P:BV + (before + 1) * P], start=(st == 0), stop=(st == t))
                    filled(ins, f"ob{t}_{before}")
            if g is None:
                return
            if c == 1:
                pe.wait_ge(acc_free, by_name["b_q"].a0 + g + 1 + FREE0)
                for t in range(TT):
                    b = use(f"qb{t}_{g}")
                    for i in range(4):
                        ins = pe.transpose(b[:, i * P:(i + 1) * P], proj[:, t, g * NB + i * P:g * NB + (i + 1) * P], ident)
                    filled(ins, f"qb{t}_{g}")
            if c in (2, 3):
                for i in ((0, 1), (2,))[c - 2]:
                    t, st = PAIRS[i]
                    wait_freed(pe, f"kb{st}")
                    wait_freed(pe, f"qb{t}_{g}")
                    filled(pe.matmul(use(f"zb{i}_{g}")[:, :], proj[:, st, BK + g * P:BK + (g + 1) * P],
                                     proj[:, t, g * NB:(g + 1) * NB], start=True, stop=True), f"zb{i}_{g}")
            if c == 6:
                pe.wait_ge(sem("softplus_masked"), 2 * g + 2)
                wait_freed(pe, f"zb1_{g}")
                summed = [unit(0)[0], unit(1)[1], unit(2)[0]]
                for i in range(3):
                    b = use(f"fb{i}_{g}")
                    ins = pe.matmul(b[:, :], const("ntri"), summed[i], start=True, stop=(i != 1))
                    if i == 1:
                        ins = pe.matmul(b[:, :], const("nones"), summed[2], start=False, stop=True)
                    filled(ins, f"fb{i}_{g}")

        def attention_b_act(act, stage, k, c):
            proj = aq["b_proj"]
            g = group_of("b_q", "b_gate", stage, k)
            if (stage, k, c) == ("b_q", 0, 1):
                for t in range(TT):
                    release(act.copy(proj[:, t, BK:BK + NB], take(act, f"kb{t}")[:, :]), f"kb{t}")
            if g is None:
                return
            if c == 1:
                for t in range(TT):
                    release(act.activation(proj[:, t, g * NB:(g + 1) * NB], take(act, f"qb{t}_{g}")[:, :], ACT.Copy,
                                           scale=float(HD) ** -0.5), f"qb{t}_{g}")
                act.preload_act_table_set("natural_log_exp_and_others")
            if c in (2, 3):
                for i in ((0, 1), (2,))[c - 2]:
                    n = 3 * (3 * g + i)
                    a_ = unit(i)[0]
                    b = take(act, f"zb{i}_{g}")
                    for func, src, scale, bias in ((ACT.Abs, b[:, :], 1.0, 0.0), (ACT.Exp, a_, -1.0, 0.0), (ACT.Ln, a_, 1.0, 1.0)):
                        act.activation(a_, src, func, scale=scale, bias=bias).then_inc(sem("stick_log"), 1)
                        n += 1
                        act.wait_ge(sem("stick_log"), n)
            if c == 7:
                for i in range(3):
                    wait_freed(act, f"fb{i}_{g}")
                    x = unit(i)[2]
                    act.activation(x, x, ACT.Exp).then_inc(sem("stick_exp"), 1)

        def attention_b_dve(dve, link, stage, k, c):
            g, before = group_of("b_q", "b_gate", stage, k), last_group(stage, k)
            if before is not None and c == 0:
                for t in range(TT):
                    release(dve.tensor_copy(tm[:, t, before * NB:(before + 1) * NB], take(dve, f"ob{t}_{before}")[:, :]), f"ob{t}_{before}")
            if g is None:
                return
            if c in (3, 4):
                for i in ((0, 1), (2,))[c - 3]:
                    lo_, sp_, x = unit(i)
                    dve.wait_ge(sem("stick_log"), 3 * (3 * g + i) + 3)
                    b = take(dve, f"zb{i}_{g}")
                    link(dve.scalar_tensor_tensor(sp_, b[:, :], 0.0, lo_, ALU.max, ALU.add))
                    release(dve.tensor_tensor(x, b[:, :], sp_, ALU.subtract), f"zb{i}_{g}")
            if c == 6:
                for i in range(3):
                    x = unit(i)[2]
                    release(dve.tensor_tensor(x, x, take(dve, f"fb{i}_{g}")[:, :], ALU.add), f"fb{i}_{g}")

        def mixer_b_pool(pool):
            strict = const("strict").unsqueeze(1).to_broadcast([P, 4, P])

            def masked(dst, src, what):
                pool.tensor_tensor(dst.rearrange("p (a b) -> p a b", a=4), src.rearrange("p (a b) -> p a b", a=4),
                                   strict, ALU.mult).then_inc(sem(what), 1)

            for g in range(KVH):
                for i in (0, 2):
                    wait_freed(pool, f"zb{i}_{g}")
                    lo_, sp_, _ = unit(i)
                    masked(lo_, sp_, "softplus_masked")
                for i in (0, 2):
                    pool.wait_ge(sem("stick_exp"), 3 * g + i + 1)
                    x = unit(i)[2]
                    masked(x, x, "weights_masked")

        def beside_pe(pe, stage, k, c):
            gla_pe(pe, stage, k, c)
            attention_a_pe(pe, stage, k, c)
            attention_b_pe(pe, stage, k, c)

        def beside_act(act, stage, k, c):
            gla_act(act, stage, k, c)
            attention_a_act(act, stage, k, c)
            attention_b_act(act, stage, k, c)

        def beside_dve(dve, link, stage, k, c):
            gla_dve(dve, link, stage, k, c)
            attention_a_dve(dve, link, stage, k, c)
            attention_b_dve(dve, link, stage, k, c)

        block = ctx.enter_context(nc.Block())

        @block.sync
        def _(sp):
            xv = A["x"].rearrange("a (t p) n -> p (a t) n", p=P)
            for k in range(4):
                sp.dma_start(h[:, :, k * NB:(k + 1) * NB], xv[:, :, k * NB:(k + 1) * NB]).then_inc(sem(f"x_in_{k}"), 16)
            for s in stages:
                w, k0, n0 = s.weights

                def load(k, u):
                    for c in range(CH):
                        tiles = s.chunk_tiles(c)
                        lo, n = k0 + tiles[0] * P, len(tiles) * P
                        sp.wait_ge(lo_done, (s.r0 + k) * CH + (c + 1))
                        col = n0 + (c // 2) * NB if s.kind == "ple" else n0 + k * NB
                        for i in range(2):
                            if s.kind == "ffn_in":
                                src = w[lo:lo + n, i, bass.ds(n0 + k * HB, HB)].rearrange("(j p) f -> p j f", p=P)
                                dst = raw[:, c, 0:2, i * HB:(i + 1) * HB]
                            elif len(tiles) == 2:
                                src = w[lo + i * P:lo + (i + 1) * P, bass.ds(col, s.width)]
                                dst = raw[:, c, i, 0:s.width]
                            else:
                                src = w[lo:lo + P, bass.ds(col + i * HB, HB)]
                                dst = raw[:, c, 0, i * HB:(i + 1) * HB]
                            sp.dma_start(dst, src).then_inc(landed[c], 16)

                paired_rounds(sp, s, load)
            view = out.rearrange("a (t p) n -> p (a t) n", p=P)
            for k in range(4):
                if last.kind == "gate":
                    sp.wait_ge(acc_free, FREE0 + last.a0 + k + 1)
                elif k == 0:
                    sp.wait_ge(acc_free, FREE0 + a)
                sp.dma_start(view[:, :, k * NB:(k + 1) * NB], h[:, :, k * NB:(k + 1) * NB]).then_inc(sem("stored"), 16)
            sp.wait_ge(sem("stored"), 64)

        @block.gpsimd
        def _(pool):
            pool.dma_start(posi[:, :], A["positions_2"].rearrange("a (t p) -> p (a t)", p=P),
                           allow_slow_non_contiguous=True).then_inc(sem("pos_in"), 16)
            pool.dma_start(ab["walpha"][0:16, :], A["w_alpha"]).then_inc(sem("pool_in"), 16)
            pool.dma_start(ab["balpha"][0:1, :], A["b_alpha"]).then_inc(sem("pool_in"), 16)
            pool.dma_start(ae["band"][:, :, :, :], A["band"]).then_inc(sem("pool_in"), 16)
            pool.dma_start(ae["wpool"][:, :, :, :], A["w_pool"].rearrange("g (c p) d -> p g c d", p=P)).then_inc(sem("pool_in"), 16)
            if "a_index" in by_name:
                pool.wait_ge(chunk_used, by_name["mix_out"].r0 * CH + 1 + USED0)
                pool.dma_start(bc[:, 0, :], A["final_norm"].partition_broadcast(P)).then_inc(sem("final_in"), 16)
            if "a_kv" in by_name:
                mixer_a_pool(pool)
            for i, nm in enumerate(("a_out", "b_out")):
                if nm not in by_name:
                    continue
                attention_done(pool, nm)
                pool.dma_start(ae["ptm"][:, :, :], A["p_2"][i].rearrange("a (t p) n -> p (a t) n", p=P)).then_inc(sem("p_in"), 16)
                pool.dma_start(bc[:, 0, :], A["ln_g_2"][i].partition_broadcast(P)).then_inc(sem(f"ln_in_{i}"), 16)
                pool.dma_start(bc[:, 1, :], A["ln_b_2"][i].partition_broadcast(P)).then_inc(sem(f"ln_in_{i}"), 16)
                if i == 0 and "b_kv" in by_name:
                    mixer_b_pool(pool)

        @block.tensor
        def _(pe):
            pe.sem_inc(chunk_used, USED0)

            def transposes(s, b, u):
                number, parity, pair, kt, gain = resolve(s, b, u)
                dst = bank[4 + parity]
                if isinstance(b, Batch):
                    issued[0] = number + 1
                if not isinstance(b, Batch) or number >= 2:
                    pe.wait_ge(t_done, number - 1)
                if emitted[4 + parity]:
                    pe.wait_ge(freed_s[4 + parity], emitted[4 + parity])
                if isinstance(b, tuple):
                    pe.wait_ge(acc_free, s.a0 + b[1] + FREE0)
                    src = [hid[:, (u - 1) % 2, t, j * P:(j + 1) * P] for j in range(2) for t in range(TT)]
                elif isinstance(b.source, tuple):
                    pe.wait_ge(acc_free, s.a0 + FREE0)
                    src = [hid[:, b.source[0], t, j * P:(j + 1) * P] for j in range(2) for t in range(TT)]
                else:
                    src = b.source(kt)
                for n, piece in enumerate(src):
                    ins = pe.transpose(dst[:, n * P:(n + 1) * P], piece, ident)
                ins.then_inc(t_full, 1)

            def middle_wait(s, k):
                if s.name == "mix_out" and k == 0:
                    for t in range(TT):
                        for j in range(2):
                            wait_freed(pe, f"og{t}{j}")
                elif s.kind == "gate" and k == 0:
                    pe.wait_ge(sem(f"normed_{s.name}"), 4)
                else:
                    pe.wait_ge(acc_free, s.a0 + k + FREE0)
                if s.kind == "ln_out" and k == 1:
                    pe.wait_ge(sem("p_in"), 16 * (1 if s.name == "a_out" else 2))

            def multiply(s, k, u, c, dst, t_first, t_last):
                tiles = s.chunk_tiles(c)
                pe.wait_ge(lo_done, (s.r0 + k) * CH + (c + 1 + LO0))
                xh, xl = pair_hi[s.pair], pair_lo[s.pair]
                for j, kt in enumerate(tiles):
                    for t in range(TT):
                        o = dst[t][:, 0:s.width]
                        wh, wl = whi[:, c % SPLIT, j, 0:s.width], wlo[:, c % SPLIT, j, 0:s.width]
                        xht, xlt = xh[:, kt, t * P:(t + 1) * P], xl[:, kt, t * P:(t + 1) * P]
                        pe.matmul(o, xht, wh, start=(kt == t_first), stop=False)
                        pe.matmul(o, xht, wl, start=False, stop=False)
                        ins = pe.matmul(o, xlt, wh, start=False, stop=(kt == t_last))
                return ins

            def prev_of(s):
                return stages[stages.index(s) - 1]

            pe.wait_ge(const_in, 16)
            pe.wait_ge(sem("vrow_in"), 96)
            filled(pe.transpose(use("vec")[:, 0:GAINS], vrow[0:GAINS, :], ident[0:GAINS, 0:GAINS]), "vec")
            for s in stages:
                if s is stages[0]:
                    for b in s.ahead:
                        if b.kt % 4 == 0:
                            pe.wait_ge(sem(f"x_in_{b.kt // 4}"), 16)
                        transposes(s, b, 0)
                elif s.kind == "gate":
                    for b in s.ahead:
                        if b.kt % 4 == 0:
                            pe.wait_ge(sem(f"normed_{s.name}"), b.kt // 4 + 1)
                        transposes(s, b, 0)

                def round_(k, u):
                    peeled = isinstance(k, int)
                    if s.kind != "ple":
                        pe.wait_ge(acc_free, s.a0 + k + 1)
                    dst = [acc_par(s, u, t) for t in range(TT)]
                    tiles = [kt for c in range(CH) for kt in s.chunk_tiles(c)]
                    for c in range(CH):
                        if c == 2 and peeled and k == 0 and s.early:
                            pe.wait_ge(sem(f"normed_{s.name}"), 3)
                            for b in s.early:
                                transposes(s, b, u)
                        if c == 4:
                            todo = batches_of(s, k, peeled)
                            if peeled and s.before.get(k):
                                middle_wait(s, k)
                            for b in todo:
                                transposes(s, b, u)
                        if s.kind == "ple":
                            j = c // 2
                            dst = [acc(s.a0 + j, t) for t in range(TT)]
                            if c % 2 == 0:
                                pe.wait_ge(acc_free, s.a0 + j + 1)
                        if peeled and k == 0:
                            if s.name == "mix_out" and c < 4:
                                pe.wait_ge(sem("pool_split"), c + 1)
                            pe.wait_ge(t_done, s.need[c])
                        ins = multiply(s, k, u, c, dst, tiles[0], 1 if s.kind == "ple" else tiles[-1])
                        ins.then_inc(chunk_used, 1)
                        if peeled:
                            beside_pe(pe, s.name, k, c)

                paired_rounds(pe, s, round_)

        @block.scalar
        def _(act):
            act.dma_start(con[:, :], A["consts"]).then_inc(const_in, 16)
            for name, row in (("ffn1_norm", 0), ("mix_norm", 16), ("ffn2_norm", 32), ("final_norm", 48),
                              ("pool_scale", 64), ("gla_norm", 72)):
                v = A[name] if len(A[name].shape) == 1 else A[name].rearrange("a n -> (a n)")
                v = v.rearrange("(r n) -> r n", n=P)
                act.dma_start(vrow[row:row + v.shape[0], :], v).then_inc(sem("vrow_in"), 16)

            def split_hi(s, k, c, n):
                act.wait_ge(landed[c], (s.r0 + k) * 32 + 32)
                act.wait_ge(chunk_used, (s.r0 + k) * CH + (c + 1))
                w = width_of(s, k)
                act.copy(whi[:, c % SPLIT, 0:n, 0:w], raw[:, c, 0:n, 0:w]).then_inc(hi_done, 1)

            def operand_hi(s, b, u):
                number, parity, pair, kt, gain = resolve(s, b, u)
                act.wait_ge(t_full, number + 1)
                src = bank[4 + parity]
                dst = pair_hi[pair]
                if gain is None:
                    act.copy(dst[:, bass.ds(kt, 2), :], src[:, :].rearrange("p (j n) -> p j n", j=2)).then_inc(t_hi, 1)
                else:
                    for j in range(2):
                        g = GAIN["gla"] + j if gain == "gla" else gain + kt + j
                        ins = act.activation(dst[:, kt + j, :], src[:, j * SEQ:(j + 1) * SEQ], ACT.Copy, scale=vec[:, g:g + 1])
                    ins.then_inc(t_hi, 1)

            squared = [0]

            def squares(blk):
                if squared[0]:
                    act.wait_ge(sem("squares_done"), squared[0])
                squared[0] += 1
                for t in range(TT):
                    ins = act.activation(sgw[:, t, :], h[:, t, blk * NB:(blk + 1) * NB], ACT.Square,
                                         accum_out=parts[:, t, blk:blk + 1])
                ins.then_inc(sem("squares_done"), 1)

            stat = [0]

            def root(n):
                act.wait_ge(sem("sumsq_done"), n + 1)
                act.activation(std, ssq, ACT.Sqrt, bias=eps_c, scale=1.0 / D).then_inc(sem("root_done"), 1)
                act.wait_ge(sem("rstd_done"), n + 1)

            def evacuate(s, k, u):
                peeled = isinstance(k, int)
                pair = [acc_par(s, u, t) for t in range(TT)]
                full_at = s.a0 + k + 1
                if s.kind == "ffn_in":
                    sums_done(act, s, k)
                    for t in range(TT):
                        ins = act.activation(sg[:, u, t, :], pair[t][:, 0:HB], ACT.Silu, scale=rstd[:, t:t + 1])
                    ins.then_inc(silu_done, 1)
                elif s.name in ("ffn1_out2", "mix_out", "ffn2_out2"):
                    act.wait_ge(acc_free, full_at + FREE0)
                    squares(k)
                elif s.kind == "project":
                    sums_done(act, s, k)
                    width = s.width
                    for t in range(TT):
                        func, dst = placed(s, k, t)
                        scale = rstd[:, t:t + 1] if s.name[0] != "b" else 1.0
                        ins = act.activation(dst, pair[t][:, 0:width], func, scale=scale)
                    ins.then_inc(acc_free, 1)
                elif s.kind in ("gate", "head_gate"):
                    sums_done(act, s, k)
                    act.wait_ge(acc_free, full_at - 1 + FREE0)
                    for t in range(TT):
                        if s.kind == "gate":
                            ins = act.activation(sgw[:, t, :], pair[t][:, :], ACT.Sigmoid)
                        else:
                            ins = act.activation(sgw[:, t, :], pair[t][:, :], ACT.Silu,
                                                 scale=rstd[:, t:t + 1] if s.name[0] == "a" else 1.0)
                    ins.then_inc(silu_done, 1)

            def placed(s, k, t):
                if s.name == "mix_decay":
                    return ACT.Copy, ab["rtm"][:, t, :]
                if s.name == "a_tail":
                    return ACT.Copy, ae["index_tail"][:, t, :]
                if s.name == "mix_gate":
                    return ACT.Silu, tm[:, t, 1024 + k * NB:1024 + (k + 1) * NB]
                buf, first = dict(mix_pool=(aq["u"], 0), mix_qk=(aq["u"], 1024), mix_v=(aq["u"], 2048),
                                  a_index=(ap["a_proj"], 3072), a_kv=(ap["a_proj"], 2048), a_q=(ap["a_proj"], 0),
                                  b_kv=(aq["b_proj"], 2048), b_q=(aq["b_proj"], 0))[s.name]
                return ACT.Copy, buf[:, t, first + k * NB:first + (k + 1) * NB]

            act.wait_ge(sem("cleared"), 1)
            act.wait_ge(sem("vrow_in"), 96)
            release(act.copy(vec[:, 0:GAINS], take(act, "vec")[:, 0:GAINS]), "vec")
            for k in range(4):
                act.wait_ge(sem(f"x_in_{k}"), 16)
                squares(k)
            s0 = stages[0]
            for c in range(4):
                split_hi(s0, 0, c, 2)
            for b in s0.ahead:
                operand_hi(s0, b, 0)
            nstat = 1
            pending_root = 0
            act.wait_ge(sem("trig_args"), 1)
            act.activation(trig[:, 3, :, :], trig[:, 2, :, :], ACT.Sin)
            act.activation(trig[:, 4, :, :], trig[:, 2, :, :], ACT.Sin, scale=0.5).then_inc(sem("trig_done"), 1)
            for n, s in enumerate(stages):
                nxt = stages[n + 1] if n + 1 < len(stages) else None
                if s is not s0:
                    for b in s.ahead:
                        operand_hi(s, b, 0)
                def second_half(k, u):
                    peeled = isinstance(k, int)
                    for c in range(4, CH):
                        split_hi(s, k, c, 1 if s.kind == "ple" or s.tiles == 12 else 2)
                        if peeled:
                            beside_act(act, s.name, k, c - 4)
                        if c == 5 and peeled and k == 0:
                            for b in s.early:
                                operand_hi(s, b, u)
                    for b in batches_of(s, k, peeled):
                        operand_hi(s, b, u)

                def first_half(k, kind, peeled):
                    for c in range(4):
                        split_hi(s, k, c, 1 if kind == "ple" else 2)
                        if peeled:
                            beside_act(act, s.name, k - 1, c + 4)

                def round_(k, u):
                    peeled = isinstance(k, int)
                    second_half(k, u)
                    if s.kind == "ple":
                        act.wait_ge(sem("mean_var_done"), 1 if s.name == "ple0" else 2)
                        act.activation(std, mv[:, :, 1], ACT.Sqrt, bias=lneps_c).then_inc(sem("ln_root_done"), 1)
                        for j in range(4):
                            act.wait_ge(chunk_used, s.r0 * CH + 2 * (j + 1) + USED0)
                            for t in range(TT):
                                ins = act.copy(tm[:, t, j * NB:(j + 1) * NB], acc(s.a0 + j, t)[:, :])
                            ins.then_inc(acc_free, 1)
                    if not (peeled and k == s.n - 1 and nxt is None):
                        first_half(k + 1, nxt.kind if peeled and k == s.n - 1 else s.kind, peeled)
                    if peeled and k == 0 and s.name in NORMED:
                        root(NORMED.index(s.name))
                    if s.kind != "ple":
                        evacuate(s, k, u)

                if s.name == "mix_out":
                    for c in range(4):
                        act.copy(pair_hi["P"][:, 2 * c:2 * c + 2, :], aq["pool_out"][:, 2 * c:2 * c + 2, :]).then_inc(sem("pool_split_hi"), 1)
                paired_rounds(act, s, round_)

        @block.vector
        def _(dve):
            dve.sem_inc(lo_done, LO0)
            dve.sem_inc(acc_free, FREE0)
            steps = sem("vector_step")
            stepped = [0]

            def link(ins):
                stepped[0] += 1
                ins.then_inc(steps, 1)
                dve.wait_ge(steps, stepped[0])

            def split_lo(s, k, c, n):
                dve.wait_ge(hi_done, (s.r0 + k) * CH + (c + 1))
                w = width_of(s, k)
                dve.tensor_tensor(wlo[:, c % SPLIT, 0:n, 0:w], raw[:, c, 0:n, 0:w], whi[:, c % SPLIT, 0:n, 0:w].bitcast(F32),
                                  ALU.subtract).then_inc(lo_done, 1)

            def operand_lo(s, b, u):
                number, parity, pair, kt, gain = resolve(s, b, u)
                dve.wait_ge(t_hi, number + 1)
                src, hi_, lo_ = bank[4 + parity], pair_hi[pair], pair_lo[pair]
                if gain is None:
                    dve.tensor_tensor(lo_[:, bass.ds(kt, 2), :], src[:, :].rearrange("p (j n) -> p j n", j=2),
                                      hi_[:, bass.ds(kt, 2), :].bitcast(F32), ALU.subtract).then_inc(t_done, 1)
                else:
                    for j in range(2):
                        g = GAIN["gla"] + j if gain == "gla" else gain + kt + j
                        ins = dve.scalar_tensor_tensor(lo_[:, kt + j, :], src[:, j * SEQ:(j + 1) * SEQ], vec[:, g:g + 1],
                                                       hi_[:, kt + j, :].bitcast(F32), ALU.mult, ALU.subtract)
                    ins.then_inc(t_done, 1)

            def rms(n):
                dve.wait_ge(sem("squares_done"), 4 * n + 4)
                dve.tensor_reduce(ssq, parts, AX.X, ALU.add).then_inc(sem("sumsq_done"), 1)
                dve.wait_ge(sem("root_done"), n + 1)
                dve.reciprocal(rstd, std).then_inc(sem("rstd_done"), 1)
                dve.wait_ge(sem("rstd_done"), n + 1)

            def evacuate(s, k, u):
                pair = [acc_par(s, u, t) for t in range(TT)]
                at_ = s.a0 + k + 1
                if s.kind == "ffn_in":
                    dve.wait_ge(silu_done, silu_before(s) + k + 1)
                    for t in range(TT):
                        ins = dve.scalar_tensor_tensor(hid[:, u, t, :], pair[t][:, HB:NB], rstd[:, t:t + 1],
                                                       sg[:, u, t, :], ALU.mult, ALU.mult)
                    ins.then_inc(acc_free, 1)
                elif s.kind in ("ffn_out", "mix_out", "ln_out"):
                    sums_done(dve, s, k)
                    for t in range(TT):
                        hb = h[:, t, k * NB:(k + 1) * NB]
                        if s.kind == "ln_out":
                            ins = dve.scalar_tensor_tensor(hb, hb, ALPHA, pair[t][:, :], ALU.mult, ALU.add)
                        else:
                            c = 0.5 if s.kind == "ffn_out" else 1.0
                            ins = dve.scalar_tensor_tensor(hb, pair[t][:, :], c, hb, ALU.mult, ALU.add)
                    ins.then_inc(acc_free, 1)
                    if s.kind == "ln_out":
                        dve.wait_ge(acc_free, at_ + FREE0)
                        for t in range(TT):
                            ins = dve.bn_stats(bn[:, t, k, :], h[:, t, k * NB:(k + 1) * NB])
                        link(ins)
                elif s.kind == "head_gate":
                    dve.wait_ge(silu_done, silu_before(s) + k + 1)
                    for t in range(TT):
                        o = tm[:, t, k * NB:(k + 1) * NB]
                        ins = dve.tensor_tensor(o, o, sgw[:, t, :], ALU.mult)
                    ins.then_inc(acc_free, 1)
                elif s.kind == "gate":
                    dve.wait_ge(silu_done, silu_before(s) + k + 1)
                    for t in range(TT):
                        ins = dve.tensor_tensor(sgw[:, t, :], sgw[:, t, :], tm[:, t, k * NB:(k + 1) * NB], ALU.mult)
                    link(ins)
                    for t in range(TT):
                        hb = h[:, t, k * NB:(k + 1) * NB]
                        ins = dve.tensor_tensor(hb, hb, sgw[:, t, :], ALU.add)
                    ins.then_inc(acc_free, 1)

            def silu_before(s):
                return sum(q.n for q in stages[:stages.index(s)] if q.kind in ("ffn_in", "gate", "head_gate"))

            def norm_block(i, gate, k):
                cols = slice(k * NB, (k + 1) * NB)
                for t in range(TT):
                    ins = dve.scalar_tensor_tensor(h[:, t, cols], h[:, t, cols], mv[:, t, 0:1], bc[:, 0, cols],
                                                   ALU.subtract, ALU.mult)
                link(ins)
                for t in range(TT):
                    ins = dve.scalar_tensor_tensor(h[:, t, cols], h[:, t, cols], rstd[:, t:t + 1], bc[:, 1, cols],
                                                   ALU.mult, ALU.add)
                ins.then_inc(sem(f"normed_{gate}"), 1)

            def layer_norm(i, gate):
                link(dve.bn_aggr(mv[:, 0, :], bn[:, 0, :, :]))
                dve.bn_aggr(mv[:, 1, :], bn[:, 1, :, :]).then_inc(sem("mean_var_done"), 1)
                dve.wait_ge(sem("ln_root_done"), i + 1)
                link(dve.reciprocal(rstd, std))
                dve.wait_ge(sem(f"ln_in_{i}"), 32)
                for k in range(3):
                    norm_block(i, gate, k)

            dve.memset(eps_c, EPS)
            dve.memset(lneps_c, LN_EPS).then_inc(sem("cleared"), 1)
            s0 = stages[0]
            for c in range(4):
                split_lo(s0, 0, c, 2)
            wait_freed(dve, "vec")
            dve.memset(vrow[:, :], 1.0).then_inc(sem("ones_done"), 1)
            for b in s0.ahead:
                operand_lo(s0, b, 0)
            angles(dve, link)
            for n, s in enumerate(stages):
                nxt = stages[n + 1] if n + 1 < len(stages) else None
                if s is not s0:
                    for b in s.ahead:
                        operand_lo(s, b, 0)
                if s.kind == "gate":
                    norm_block(0 if s.name == "gate0" else 1, s.name, 3)
                if s.name == "mix_out":
                    gla_heads_out(dve, 1)
                    for c in range(4):
                        dve.wait_ge(sem("pool_split_hi"), c + 1)
                        dve.tensor_tensor(pair_lo["P"][:, 2 * c:2 * c + 2, :], aq["pool_out"][:, 2 * c:2 * c + 2, :],
                                          pair_hi["P"][:, 2 * c:2 * c + 2, :].bitcast(F32), ALU.subtract).then_inc(sem("pool_split"), 1)

                def round_(k, u):
                    peeled = isinstance(k, int)
                    for c in range(4, CH):
                        split_lo(s, k, c, 1 if s.kind == "ple" or s.tiles == 12 else 2)
                        if peeled:
                            beside_dve(dve, link, s.name, k, c - 4)
                        if c == 5 and peeled and k == 0:
                            for b in s.early:
                                operand_lo(s, b, u)
                    for b in batches_of(s, k, peeled):
                        operand_lo(s, b, u)
                    if s.kind == "ple":
                        layer_norm(0 if s.name == "ple0" else 1, "gate0" if s.name == "ple0" else "gate1")
                    if not (peeled and k == s.n - 1 and nxt is None):
                        kind = nxt.kind if peeled and k == s.n - 1 else s.kind
                        for c in range(4):
                            split_lo(s, k + 1, c, 1 if kind == "ple" else 2)
                            if peeled:
                                beside_dve(dve, link, s.name, k, c + 4)
                    if peeled and k == 0 and s.name in NORMED:
                        rms(NORMED.index(s.name))
                    evacuate(s, k, u)

                paired_rounds(dve, s, round_)
    return stages


_INS = ['x', 'ffn1_norm', 'ffn1_w_in', 'ffn1_w_out', 'mix_norm', 'w_in_mix', 'w_pool', 'pool_scale', 'w_alpha',
        'b_alpha', 'gla_norm', 'w_out_mix', 'ffn2_norm', 'ffn2_w_in', 'ffn2_w_out', 'final_norm', 'p_2',
        'positions_2', 'w_in_a_2', 'w_o_a_2', 'w_kv_b_2', 'w_in_b_2', 'w_o_b_2', 'ln_g_2', 'ln_b_2', 'w_ple_2',
        'w_ple_gate_2']
_ONE_LAYER = {'ffn1_w_in', 'ffn1_w_out', 'w_in_mix', 'w_pool', 'w_alpha', 'w_out_mix', 'ffn2_w_in', 'ffn2_w_out',
              'w_in_a_2', 'w_o_a_2', 'w_in_b_2', 'w_o_b_2'}


def kernel(**inputs):
    import numpy as _np
    import concourse.bacc as _bacc
    from concourse import mybir as _mybir
    from concourse.bass_utils import run_bass_kernel_spmd as _run

    nc = _bacc.Bacc("TRN2", target_bir_lowering=False, num_devices=1)
    given = {name: _np.ascontiguousarray(inputs[name]) for name in _INS}
    given["consts"], given["band"] = shape_constants()
    arrays, args = {}, {}
    for name, a in given.items():
        arrays[f"in_{name}_dram"] = a
        ap = nc.dram_tensor(f"in_{name}_dram", a.shape, _mybir.dt.from_np(a.dtype), kind="ExternalInput").ap()
        args[name] = ap[0] if name in _ONE_LAYER else ap
    out = nc.dram_tensor("out_0_dram", (1, SEQ, D), _mybir.dt.float32, kind="ExternalOutput").ap()
    build(nc, args, out)
    return _run(nc, [arrays], core_ids=[0]).results[0]["out_0_dram"]
```

```python
from contextlib import ExitStack

import numpy as np

import concourse.bass as bass
from concourse import mybir

F32 = mybir.dt.float32
F32R = mybir.dt.float32r
I32 = mybir.dt.int32
ALU = mybir.AluOpType
ACT = mybir.ActivationFunctionType
AX = mybir.AxisListType

P = 128
SEQ = 256
TT = SEQ // P
D = 2048
KT = D // P
FF = 5632
NB = 512
HB = NB // 2
CH = 8
SPLIT = 4
EPS = 1e-6
LN_EPS = 1e-5
ALPHA = 4.0 ** 0.25
POOLS = (2, 4, 8, 16)
GH, GDK, GDV, CHUNK = 4, 128, 256, 64
KVH, HD = 4, 128
IH, ID = 16, 64
NSEL = 64
ROT, IROT = 16, 8
FAR = -3.0e38
TAKEN = -3.4e38
MAGIC = 1.5 * 2.0 ** 23
PI = 3.14159265
TWO_PI = (6.28125, 1.9350051879882812e-3, 3.0198e-7)
GAINS = 74
NORMED = ["ffn1_in0", "mix_pool", "ffn2_in0", "a_index"]
CONST = dict(ident=0, tri16=1, suf16=2, causal=3, strict=4, ntri=5, nones=6)


def shape_constants():
    i, j = np.arange(P)[:, None], np.arange(P)[None, :]
    same = (i // CHUNK) == (j // CHUNK)
    mats = [
        i == j,
        (same & (i <= j)) / 16.0,
        (same & (i > j)) / 16.0,
        same & (i <= j),
        i < j,
        -1.0 * (i > j),
        -np.ones((P, P)),
    ]
    inv_q = 1.0 / (500000.0 ** (np.arange(ROT) / ROT))
    inv_i = 1.0 / (500000.0 ** (np.arange(IROT) / IROT))
    rows = np.broadcast_to(np.concatenate([inv_q, inv_i]), (P, ROT + IROT))
    consts = np.concatenate([np.asarray(m, np.float32) for m in mats] + [rows], axis=1)
    s, t = np.arange(SEQ)[:, None], np.arange(SEQ)[None, :]
    band = [((t - s >= 0) & (t - s < w)) / np.minimum(t + 1, w) - (s == t) for w in POOLS]
    band = np.stack(band).reshape(len(POOLS), TT, P, SEQ).transpose(2, 0, 1, 3)
    return np.ascontiguousarray(consts, np.float32), np.ascontiguousarray(band, np.float32)


class Stage:

    def __init__(self, name, kind, n, tiles, pair, weights, width=NB):
        self.name, self.kind, self.n, self.tiles = name, kind, n, tiles
        self.pair, self.weights, self.width = pair, weights, width
        self.r0 = self.a0 = 0
        self.before = {}
        self.ahead = []
        self.mid = {}
        self.late = False
        self.need = {}

    def chunk_tiles(self, c):
        if self.kind == "ple":
            return [c % 2]
        if self.tiles == KT:
            return [2 * c, 2 * c + 1]
        return [2 * c, 2 * c + 1] if c < 4 else [4 + c]


class Batch:

    def __init__(self, source, pair, kt, gain=None):
        self.source, self.pair, self.kt, self.gain = source, pair, kt, gain
        self.number = None


def paired_rounds(eng, stage, body):
    first = min(stage.n, 2) if stage.n > 4 else stage.n
    for k in range(first):
        body(k, k)
    if stage.n > first:
        with eng.Fori(0, (stage.n - first) // 2) as i:
            for u in range(2):
                body(i * 2 + (first + u), u)


def build(nc, A, out, upto=None):
    ctx = ExitStack()
    with ctx:
        def sb(name, shape, dt=F32):
            return ctx.enter_context(nc.sbuf_tensor(name, shape, dt))

        def overlaid(*groups):
            made = {}
            longest = max(groups, key=lambda g: sum(int(np.prod(s[1:])) for _, s, _ in g))
            for g in groups:
                if g is longest:
                    continue
                with ExitStack() as local:
                    for n, s, dt in g:
                        made[n] = local.enter_context(nc.sbuf_tensor(n, s, dt))
            for n, s, dt in longest:
                made[n] = sb(n, s, dt)
            return made

        sems = {}

        def sem(name):
            if name not in sems:
                sems[name] = ctx.enter_context(nc.semaphore(name))
            return sems[name]

        raw = sb("raw", [P, CH, 2, NB])
        whi = sb("whi", [P, SPLIT, 2, NB], F32R)
        wlo = sb("wlo", [P, SPLIT, 2, NB], F32R)
        ap = overlaid([("p_hi", [P, KT, SEQ], F32R), ("p_lo", [P, KT, SEQ], F32R)],
                      [("a_proj", [P, TT, 4096], F32)])
        aq = overlaid([("q_hi", [P, KT, SEQ], F32R), ("q_lo", [P, KT, SEQ], F32R)],
                      [("u", [P, TT, 3072], F32), ("pool_out", [P, 8, SEQ], F32)],
                      [("b_proj", [P, TT, 3072], F32), ("unit_q", [P, 4, NB], F32)])
        pair_hi = dict(P=ap["p_hi"], Q=aq["q_hi"])
        pair_lo = dict(P=ap["p_lo"], Q=aq["q_lo"])
        h = sb("h", [P, TT, D])
        at = overlaid([("tm", [P, TT, D], F32)], [("hid", [P, 2, TT, HB], F32)])
        tm, hid = at["tm"], at["hid"]
        ab = overlaid([("bc", [P, 2, D], F32)],
                      [("pooled", [P, 2, 2, SEQ], F32), ("walpha", [P, NB], F32),
                       ("balpha", [P, NB], F32), ("rt", [P, SEQ], F32), ("rtm", [P, TT, 16], F32)],
                      [("prob0", [P, 4, P], F32), ("prob1", [P, 4, SEQ], F32), ("probt", [P, 3, NB], F32)])
        bc = ab["bc"]
        sg = sb("sg", [P, 2, TT, HB])
        sgw = sg[:, :, :, :].rearrange("p a t n -> p a (t n)")
        ae = overlaid([("band", [P, 4, TT, SEQ], F32), ("wpool", [P, 4, 2, SEQ], F32), ("ex", [P, TT, NB], F32)],
                      [("state", [P, 3, GH * GDV], F32), ("scm", [P, TT, NB], F32)],
                      [("index_tail", [P, TT, 80], F32), ("isc", [P, TT, SEQ], F32), ("iwork", [P, TT, SEQ], F32),
                       ("amask", [P, TT, SEQ], F32), ("ikd", [P, TT, P], F32), ("ikt", [P, SEQ], F32),
                       ("kt_a", [P, KVH, SEQ], F32), ("rope_a", [P, 4, 4 * ROT], F32), ("rope_b", [P, 4, IH * IROT], F32)],
                      [("unit_e", [P, 5, NB], F32), ("unit_pad", [P, 1536], F32), ("ptm", [P, TT, SEQ], F32)],
                      [("pt_hi_pad", [P, TT, 1280], F32), ("pt_hi", [P, 2, SEQ], F32R),
                       ("pt_lo", [P, 2, SEQ], F32R)])
        pair_hi["E"], pair_lo["E"] = ae["pt_hi"], ae["pt_lo"]
        con = sb("con", [P, 7 * P + ROT + IROT])
        vrow = sb("vrow", [P, P])
        vec = sb("vec", [P, P])
        posi = sb("posi", [P, TT], I32)
        trig = sb("trig", [P, 6, TT, ROT + IROT])
        small = sb("small", [P, 96])
        bn = sb("bn", [P, TT, 4, 6])
        rsum = sb("rsum", [P, 8, 4])

        def const(name):
            return con[:, CONST[name] * P:(CONST[name] + 1) * P]

        ident = const("ident")
        parts = small[:, 0:8].rearrange("p (t n) -> p t n", t=TT)
        ssq, std, rstd = small[:, 8:10], small[:, 10:12], small[:, 12:14]
        eps_c, lneps_c, one_c = small[:, 14:15], small[:, 15:16], small[:, 16:17]
        mv = small[:, 18:22].rearrange("p (t n) -> p t n", t=TT)
        oss, ostd, orstd = small[:, 24:32], small[:, 32:40], small[:, 40:48]
        top8 = small[:, 48:56]
        nmax = small[:, 56:72].rearrange("p (b n) -> p b n", b=4)

        bank = [ctx.enter_context(nc.psum_tensor(f"bank{b}", [P, NB], F32)) for b in range(8)]
        MB = [6, 7, 4, 5]

        def ffn(tag, w_in, w_out, xs, hs):
            w3 = w_in.rearrange("k (s f) -> k s f", s=2)
            got, f0 = [], 0
            for g, n in enumerate((8, 8, 6)):
                got.append(Stage(f"{tag}_in{g}", "ffn_in", n, KT, xs, (w3, 0, f0)))
                got.append(Stage(f"{tag}_out{g}", "ffn_out", 4, 2 * n, hs, (w_out, f0, 0)))
                f0 += n * HB
            return got

        W = A
        stages = ffn("ffn1", W["ffn1_w_in"], W["ffn1_w_out"], "P", "Q")
        M, A1, B1 = W["w_in_mix"], W["w_in_a_2"], W["w_in_b_2"]
        stages += [Stage("mix_pool", "project", 2, KT, "P", (M, 0, 0)),
                   Stage("mix_decay", "narrow", 1, KT, "P", (M, 0, 4096), 16),
                   Stage("mix_qk", "project", 2, KT, "P", (M, 0, 1024)),
                   Stage("mix_v", "project", 2, KT, "P", (M, 0, 2048)),
                   Stage("mix_gate", "project", 2, KT, "P", (M, 0, 3072)),
                   Stage("mix_out", "mix_out", 4, KT, "P", (W["w_out_mix"], 0, 0))]
        stages += ffn("ffn2", W["ffn2_w_in"], W["ffn2_w_out"], "Q", "P")
        stages += [Stage("a_index", "project", 2, KT, "Q", (A1, 0, 5120)),
                   Stage("a_tail", "narrow", 1, KT, "Q", (A1, 0, 6144), 80),
                   Stage("a_kv", "project", 2, KT, "Q", (A1, 0, 2048)),
                   Stage("a_q", "project", 4, KT, "Q", (A1, 0, 0)),
                   Stage("a_gate", "head_gate", 4, KT, "Q", (A1, 0, 3072)),
                   Stage("a_out", "ln_out", 4, KT, "P", (W["w_o_a_2"], 0, 0)),
                   Stage("ple0", "ple", 1, 2, "E", (W["w_ple_2"][0], 0, 0)),
                   Stage("gate0", "gate", 4, KT, "Q", (W["w_ple_gate_2"][0], 0, 0)),
                   Stage("b_kv", "project", 2, KT, "P", (W["w_kv_b_2"], 0, 0)),
                   Stage("b_q", "project", 4, KT, "P", (B1, 0, 0)),
                   Stage("b_gate", "head_gate", 4, KT, "P", (B1, 0, 2048)),
                   Stage("b_out", "ln_out", 4, KT, "Q", (W["w_o_b_2"], 0, 0)),
                   Stage("ple1", "ple", 1, 2, "E", (W["w_ple_2"][1], 0, 0)),
                   Stage("gate1", "gate", 4, KT, "P", (W["w_ple_gate_2"][1], 0, 0))]
        if upto is not None:
            stages = stages[:[s.name for s in stages].index(upto) + 1]
        by_name = {s.name: s for s in stages}
        r = a = 0
        for s in stages:
            s.r0, s.a0 = r, a
            r, a = r + s.n, a + (4 if s.kind == "ple" else s.n)
        last = stages[-1]

        GAIN = dict(ffn1=0, mix=16, ffn2=32, final=48, pool=64, gla=72)

        def columns(buf, kt0=0):
            return lambda kt: [buf[:, t, (kt - kt0 + j) * P:(kt - kt0 + j + 1) * P] for j in range(2) for t in range(TT)]

        follows = {"ffn1_out2": ("P", "mix"), "mix_out": ("Q", "ffn2"), "ffn2_out2": ("Q", "final"), "gate0": ("P", None)}
        for n, s in enumerate(stages):
            nxt = stages[n + 1] if n + 1 < len(stages) else None
            if n == 0:
                made = [Batch(columns(h), "P", kt, GAIN["ffn1"]) for kt in range(0, KT, 2)]
                s.ahead, s.mid = made[:2], {c: [made[c + 2]] for c in range(CH - 2)}
            if s.name == "mix_out":
                made = [Batch(columns(tm, 8), "P", kt, "gla") for kt in range(8, KT, 2)]
                s.mid, s.late = {3: made[:2], 4: made[2:3], 5: made[3:]}, True
            if s.kind == "ln_out":
                s.before.setdefault(1, []).append(Batch(columns(ae["ptm"]), "E", 0))
            if s.kind == "head_gate" and nxt:
                for k, blocks in ((2, (0, 1)), (3, (2,)), (4, (3,))):
                    where = s.before if k < s.n else nxt.before
                    where.setdefault(k % s.n, []).extend(
                        Batch(columns(tm), nxt.pair, 4 * blk + 2 * j) for blk in blocks for j in range(2))
            if s.kind == "gate":
                made = [Batch(columns(h), s.pair, kt) for kt in range(0, KT, 2)]
                stages[n - 1].mid = {6: made[:2]}
                s.mid = {1: made[2:4], 3: made[4:6], 5: made[6:8]}
            if s.kind == "ffn_in" and nxt:
                s.hid_pair = nxt.pair
                nxt.before.setdefault(0, []).append(Batch(((s.n - 1) % 2,), nxt.pair, 2 * (s.n - 1)))
            if s.name in follows and nxt:
                pair, gain = follows[s.name]
                for k in range(s.n):
                    where = s.before if k + 1 < s.n else nxt.before
                    where.setdefault((k + 1) % s.n, []).extend(
                        Batch(columns(h), pair, 4 * k + 2 * j, GAIN[gain] if gain else None) for j in range(2))
        n, latest = 0, {}
        for s in stages:
            for b in s.ahead:
                b.number, latest[b.pair, b.kt], n = n, n, n + 1
            for k in range(s.n):
                for c in range(CH):
                    if k == 0:
                        for b in s.mid.get(c, []):
                            b.number, latest[b.pair, b.kt], n = n, n, n + 1
                    if c == 4:
                        for b in s.before.get(k, []):
                            b.number, latest[b.pair, b.kt], n = n, n, n + 1
                        if s.kind == "ffn_in" and k:
                            if k == 1:
                                s.hid_batch0 = n
                            latest[s.hid_pair, 2 * (k - 1)], n = n, n + 1
                    if k == 0:
                        s.need[c] = latest[s.pair, s.chunk_tiles(c)[-1] // 2 * 2] + 1

        def batches_of(s, k, peeled):
            got = list(s.before.get(k, [])) if peeled else []
            if s.kind == "ffn_in" and not (peeled and k == 0):
                got.append(("hid", k))
            return got

        def resolve(s, b, u):
            if isinstance(b, Batch):
                return b.number, b.number % 2, b.pair, b.kt, b.gain
            k = b[1]
            return k - 1 + s.hid_batch0, (u - 1 + s.hid_batch0) % 2, s.hid_pair, (k - 1) * 2, None

        def acc(a, t):
            return bank[(a % 2) * 2 + t]

        def acc_par(s, u, t):
            return bank[((s.a0 + u) % 2) * 2 + t]

        uses, count = {}, {b: 0 for b in range(8)}

        def plan(name, m):
            b = MB[m]
            uses[name] = (b, count[b])
            count[b] += 1

        plan("vec", 0)
        plan("gains", 0)
        if "mix_qk" in by_name:
            for name, m in (("sum0", 0), ("rB", 2), ("sum1", 1), ("y0", 2), ("sum2", 0), ("y1", 3), ("sum3", 1), ("y2", 2), ("y3", 3),
                            ("rT", 0), ("z0", 0), ("z1", 1), ("b0", 0), ("suf0", 2), ("b1", 1), ("suf1", 3),
                            ("qT0", 0), ("kT0", 2), ("qT1", 1), ("kT1", 3), ("sc0", 0), ("sc1", 1),
                            ("kv00", 2), ("kv01", 3), ("kv10", 0), ("kv11", 1), ("kv20", 2), ("kv21", 3),
                            ("og00", 0), ("og01", 1), ("og10", 2), ("og11", 3)):
                plan(name, m)
        if "a_kv" in by_name:
            plan("tail", 3)
            for n, name in enumerate(("ik", "iq00", "iq01", "iq10", "iq11")):
                plan(name, n % 4)
            for n in range(16):
                plan(f"x{n}", n % 4)
            for t in range(TT):
                plan(f"ka{t}", t)
            for g in range(KVH):
                for name, m in (("qa0", 0), ("qa1", 1), ("l0", 2), ("l10", 3), ("l11", 0), ("pt0", 1), ("pt10", 2), ("pt11", 3),
                                ("oa0", 0), ("oa1", 1)):
                    plan(f"{name}_{g}", m)
        if "b_kv" in by_name:
            for t in range(TT):
                plan(f"kb{t}", t)
            for g in range(KVH):
                for name, m in (("qb0", 0), ("qb1", 1), ("ob0", 2), ("ob1", 3), ("zb0", 0), ("zb1", 1), ("zb2", 2),
                                ("fb0", 3), ("fb1", 0), ("fb2", 1)):
                    if name[0] != "o":
                        plan(f"{name}_{g}", m)
                    elif g:
                        plan(f"{name}_{g - 1}", m)
            for name, m in (("ob0", 2), ("ob1", 3)):
                plan(f"{name}_{KVH - 1}", m)

        full = [sem(f"bank_full_{b}") for b in range(8)]
        freed_s = [sem(f"bank_freed_{b}") for b in range(8)]

        emitted = {b: 0 for b in range(8)}
        issued = [0]

        def use(name):
            b, n = uses[name]
            assert emitted[b] == n, name
            emitted[b] += 1
            if n:
                nc.tensor.wait_ge(freed_s[b], n)
            if b in (4, 5) and issued[0]:
                nc.tensor.wait_ge(t_done, issued[0])
            return bank[b]

        def filled(ins, name):
            ins.then_inc(full[uses[name][0]], 1)

        def take(eng, name):
            b, n = uses[name]
            eng.wait_ge(full[b], n + 1)
            return bank[b]

        def release(ins, name):
            ins.then_inc(freed_s[uses[name][0]], 1)

        def wait_freed(eng, name):
            b, n = uses[name]
            eng.wait_ge(freed_s[b], n + 1)

        landed = [sem(f"weights_landed_{c}") for c in range(CH)]
        hi_done, lo_done, chunk_used = sem("weights_hi_done"), sem("weights_lo_done"), sem("chunk_used")
        acc_free = sem("acc_free")
        t_full, t_hi, t_done = sem("transposed"), sem("operand_hi_done"), sem("operand_done")
        silu_done = sem("silu_done")
        ident_in, const_in = sem("ident_in"), sem("const_in")

        LO0, USED0, FREE0 = CH, SPLIT, 2

        def round_before(s, k):
            if k:
                return s.name, k - 1
            q = stages[stages.index(s) - 1]
            return q.name, q.n - 1

        def sums_done(eng, s, k):
            eng.wait_ge(chunk_used, (s.r0 + k) * CH + (CH + USED0))

        def attention_done(eng, stage):
            for t in range(TT):
                wait_freed(eng, f"{'oa' if stage == 'a_out' else 'ob'}{t}_{KVH - 1}")

        def angles(dve, link):
            posf = small[:, 72:74]
            dve.wait_ge(sem("pos_in"), 16)
            dve.wait_ge(const_in, 16)
            link(dve.tensor_copy(posf, posi[:, :]))
            ang, turns, left = (trig[:, i, :, :] for i in range(3))
            for t in range(TT):
                ins = dve.tensor_scalar(trig[:, 0, t, :], con[:, 7 * P:7 * P + ROT + IROT], posf[:, t:t + 1], None, ALU.mult)
            link(ins)
            link(dve.tensor_scalar(turns, ang, 1.0 / (2.0 * np.pi), MAGIC, ALU.mult, ALU.add))
            link(dve.tensor_scalar(turns, turns, MAGIC, None, ALU.subtract))
            link(dve.scalar_tensor_tensor(left, turns, -TWO_PI[0], ang, ALU.mult, ALU.add))
            for part in TWO_PI[1:]:
                link(dve.scalar_tensor_tensor(left, turns, -part, left, ALU.mult, ALU.add))
            dve.tensor_scalar(left, left, PI, -PI, ALU.min, ALU.max).then_inc(sem("trig_args"), 1)

        UQ, UK, UV = 1024, 1536, 2048

        def cols(t, first, n=P):
            return aq["u"][:, t, first:first + n]

        def narrow_back(pe, src, w, name):
            b = use(name)
            for t in range(TT):
                ins = pe.transpose(b[:, t * w:(t + 1) * w], src[0:w, t * P:(t + 1) * P], ident[0:w, 0:w])
            filled(ins, name)

        def narrow_normed(act, dst, w, name):
            b = take(act, name)
            for t in range(TT):
                ins = act.activation(dst[:, t, :], b[:, t * w:(t + 1) * w], ACT.Copy, scale=rstd[:, t:t + 1])
            release(ins, name)

        def gla_pe(pe, stage, k, c):
            u, pooled, band, wpool = aq["u"], ab["pooled"], ae["band"], ae["wpool"]
            la, kinv = tm[:, :, 1024:1536], tm[:, :, 1536:2048]

            def pool_sums(g):
                b = use(f"sum{g}")
                for j in range(2):
                    x = (2 * g + j) * P
                    pe.matmul(b[:, j * SEQ:(j + 1) * SEQ], u[:, 0, x:x + P], band[:, g, 0, :], start=True, stop=False)
                    ins = pe.matmul(b[:, j * SEQ + P:(j + 1) * SEQ], u[:, 1, x:x + P], band[:, g, 1, P:SEQ], start=False, stop=True)
                filled(ins, f"sum{g}")

            def pool_maps(g):
                wait_freed(pe, f"sum{g}")
                b = use(f"y{g}")
                for j in range(2):
                    for i in range(2):
                        ins = pe.matmul(b[:, j * SEQ:(j + 1) * SEQ], wpool[:, g, i, j * P:(j + 1) * P],
                                        pooled[:, g % 2, i, :], start=(i == 0), stop=(i == 1))
                filled(ins, f"y{g}")

            def chunk_states(n):
                t, half = n // 2, n % 2
                rows = slice(half * CHUNK, (half + 1) * CHUNK)
                pe.wait_ge(sem("ktail_done"), t + 1)
                for j in range(2):
                    b = use(f"kv{n}{j}")
                    for hd in (2 * j, 2 * j + 1):
                        ins = pe.matmul(b[:, (hd % 2) * GDV:(hd % 2 + 1) * GDV], u[rows, t, UK + hd * P:UK + (hd + 1) * P],
                                        u[rows, t, UV + hd * GDV:UV + (hd + 1) * GDV], start=True, stop=True)
                    filled(ins, f"kv{n}{j}")

            def outputs(t):
                for j in range(2):
                    b = use(f"og{t}{j}")
                    for n in ((0,), (1, 2))[t]:
                        wait_freed(pe, f"kv{n}{j}")
                    for hd in (2 * j, 2 * j + 1):
                        o = slice((hd % 2) * GDV, (hd % 2 + 1) * GDV)
                        ins = pe.matmul(b[:, o], ae["scm"][:, t, hd * P:(hd + 1) * P], cols(t, UV + hd * GDV, GDV), start=True, stop=False,
                                        skip_group_check=True)
                        for half in range(2):
                            n = 2 * t + half
                            if n:
                                ins = pe.matmul(b[half * CHUNK:(half + 1) * CHUNK, o], cols(t, UQ + hd * P + half * CHUNK, CHUNK),
                                                ae["state"][:, n - 1, hd * GDV:(hd + 1) * GDV], start=False, stop=True,
                                                skip_group_check=True)
                    filled(ins, f"og{t}{j}")

            step = (stage, k, c)
            if step == ("mix_qk", 0, 0):
                pe.wait_ge(sem("pool_in"), 64)
                pe.wait_ge(sem("ones_done"), 1)
                pe.wait_ge(const_in, 16)
                pe.wait_ge(acc_free, by_name["mix_decay"].a0 + 1 + FREE0)
                pool_sums(0)
                narrow_back(pe, ab["rt"], 16, "rB")
            elif stage == "mix_qk" and k == 0 and c in (1, 2, 3):
                pool_sums(c)
                pool_maps(c - 1)
            elif step == ("mix_qk", 0, 4):
                pool_maps(3)
                wait_freed(pe, "rB")
                b = use("rT")
                for t in range(TT):
                    ins = pe.transpose(b[0:16, t * P:(t + 1) * P], ab["rtm"][:, t, :], ident)
                filled(ins, "rT")
            elif step == ("mix_qk", 0, 5):
                wait_freed(pe, "rT")
                for t in range(TT):
                    b = use(f"z{t}")
                    pe.matmul(b[:, :], ab["rt"][0:16, t * P:(t + 1) * P], ab["walpha"][0:16, :], start=True, stop=False)
                    filled(pe.matmul(b[:, :], vrow[0:1, :], ab["balpha"][0:1, :], start=False, stop=True), f"z{t}")
            elif step == ("mix_qk", 1, 1):
                for t in range(TT):
                    wait_freed(pe, f"z{t}")
                    b = use(f"b{t}")
                    for hd in range(GH):
                        ins = pe.matmul(b[:, hd * P:(hd + 1) * P], la[:, t, hd * P:(hd + 1) * P], const("tri16"), start=True, stop=True)
                    filled(ins, f"b{t}")
                    filled(pe.matmul(use(f"suf{t}")[:, :], const("suf16"), la[:, t, :], start=True, stop=True), f"suf{t}")
            elif step == ("mix_v", 0, 1):
                pe.wait_ge(acc_free, by_name["mix_qk"].a0 + 2 + FREE0)
                for t in range(TT):
                    for name, first in (("qT", UQ), ("kT", UK)):
                        b = use(f"{name}{t}")
                        for hd in range(GH):
                            ins = pe.transpose(b[:, hd * P:(hd + 1) * P], cols(t, first + hd * P), ident)
                        filled(ins, f"{name}{t}")
            elif step == ("mix_v", 0, 5):
                for t in range(TT):
                    wait_freed(pe, f"qT{t}")
                    wait_freed(pe, f"kT{t}")
                    b = use(f"sc{t}")
                    for hd in range(GH):
                        ins = pe.matmul(b[:, hd * P:(hd + 1) * P], kinv[:, t, hd * P:(hd + 1) * P], cols(t, UQ + hd * P), start=True, stop=True)
                    filled(ins, f"sc{t}")
            elif step == ("mix_gate", 0, 1):
                pe.wait_ge(acc_free, by_name["mix_v"].a0 + 2 + FREE0)
                chunk_states(0)
            elif step == ("mix_gate", 0, 2):
                wait_freed(pe, "sc0")
                wait_freed(pe, "sc1")
                chunk_states(1)
            elif step == ("mix_gate", 0, 4):
                chunk_states(2)
            elif step == ("mix_gate", 0, 6):
                outputs(0)
            elif step == ("mix_gate", 0, 7):
                outputs(1)

        def gla_act(act, stage, k, c):
            pooled, ex, soft = ab["pooled"], ae["ex"], tm[:, :, 1536:2048]
            up, down = aq["u"][:, :, 0:512], aq["u"][:, :, 512:1024]
            step = (stage, k, c)
            if step == ("mix_qk", 0, 0):
                narrow_normed(act, ab["rtm"], 16, "rB")
            if stage == "mix_qk" and k == 0 and c < 4:
                release(act.copy(pooled[:, c % 2, :, :], take(act, f"sum{c}")[:, :].rearrange("p (i n) -> p i n", i=2)), f"sum{c}")
            elif step == ("mix_qk", 0, 4):
                release(act.copy(ab["rt"][0:16, :], take(act, "rT")[0:16, 0:SEQ]), "rT")
            elif step == ("mix_qk", 0, 5):
                act.preload_act_table_set("natural_log_exp_and_others")
                n = 0
                for t in range(TT):
                    b = take(act, f"z{t}")
                    for src, func, scale, bias, dst in ((b[:, :], ACT.Abs, 1.0, 0.0, ex[:, t, :]), (ex[:, t, :], ACT.Exp, -1.0, 0.0, ex[:, t, :]),
                                                        (ex[:, t, :], ACT.Ln, 1.0, 1.0, soft[:, t, :])):
                        if n:
                            act.wait_ge(sem("softplus_step"), n)
                        act.activation(dst, src, func, scale=scale, bias=bias).then_inc(sem("softplus_step"), 1)
                        n += 1
            elif step == ("mix_qk", 1, 1):
                for t in range(TT):
                    b = take(act, f"b{t}")
                    act.activation(up[:, t, :], b[:, :], ACT.Exp)
                    release(act.activation(down[:, t, :], b[:, :], ACT.Exp, scale=-1.0), f"b{t}")
                    release(act.activation(ex[:, t, :], take(act, f"suf{t}")[:, :], ACT.Exp), f"suf{t}")
            elif stage == "mix_gate" and k == 1 and c >= 4:
                kt = 2 * (c - 4)
                act.copy(pair_hi["P"][:, kt:kt + 2, :], aq["pool_out"][:, kt:kt + 2, :]).then_inc(sem("pool_split_hi"), 1)
            elif step == ("mix_gate", 0, 7):
                act.wait_ge(sem("ktail_done"), 2)
                for t in range(TT):
                    for j in range(2):
                        b = take(act, f"og{t}{j}")
                        for i in range(2):
                            hd = 2 * j + i
                            sink = (ex, down)[t][:, j, i * GDV:(i + 1) * GDV]
                            ins = act.activation(sink, b[:, i * GDV:(i + 1) * GDV], ACT.Square,
                                                 accum_out=oss[:, t * 4 + hd:t * 4 + hd + 1])
                ins.then_inc(sem("head_squares"), 1)
                act.wait_ge(sem("head_squares"), 1)
                act.activation(ostd, oss, ACT.Sqrt, bias=eps_c, scale=1.0 / GDV).then_inc(sem("head_root"), 1)

        def gla_heads_out(dve, j):
            dve.wait_ge(acc_free, by_name["mix_gate"].a0 + j + 1 + FREE0)
            for t in range(TT):
                b = take(dve, f"og{t}{j}")
                for i in range(2):
                    hd = 2 * j + i
                    v_ = slice(hd * GDV, (hd + 1) * GDV)
                    ins = dve.scalar_tensor_tensor(tm[:, t, v_], b[:, i * GDV:(i + 1) * GDV], orstd[:, t * 4 + hd:t * 4 + hd + 1],
                                                   tm[:, t, 1024 + hd * GDV:1024 + (hd + 1) * GDV], ALU.mult, ALU.mult)
                release(ins, f"og{t}{j}")

        def gla_dve(dve, link, stage, k, c):
            scm, ex, state = ae["scm"], ae["ex"], ae["state"]
            up, down = aq["u"][:, :, 0:512], aq["u"][:, :, 512:1024]
            la, soft = tm[:, :, 1024:1536], tm[:, :, 1536:2048]
            step = (stage, k, c)
            if stage == "mix_qk" and k == 0 and 1 <= c <= 4:
                g = c - 1
                b = take(dve, f"y{g}")
                for j in range(2):
                    s_ = GAIN["pool"] + 2 * g + j
                    ins = dve.tensor_scalar(aq["pool_out"][:, 2 * g + j, :], b[:, j * SEQ:(j + 1) * SEQ], vec[:, s_:s_ + 1], None, ALU.mult)
                release(ins, f"y{g}")
            elif step == ("mix_qk", 0, 7):
                for t in range(TT):
                    dve.wait_ge(sem("softplus_step"), 3 * (t + 1))
                    release(dve.scalar_tensor_tensor(la[:, t, :], take(dve, f"z{t}")[:, :], 0.0, soft[:, t, :], ALU.min, ALU.subtract), f"z{t}")
            elif step == ("mix_qk", 1, 4):
                dve.memset(scm[:, :, :], 0.0).then_inc(sem("scores_cleared"), 1)
            elif stage == "mix_v" and k == 0 and c in (1, 2):
                t = c - 1
                wait_freed(dve, f"b{t}")
                release(dve.scalar_tensor_tensor(cols(t, UQ, NB), take(dve, f"qT{t}")[:, :], float(GDK) ** -0.5, up[:, t, :], ALU.mult, ALU.mult), f"qT{t}")
                release(dve.tensor_tensor(soft[:, t, :], take(dve, f"kT{t}")[:, :], down[:, t, :], ALU.mult), f"kT{t}")
                wait_freed(dve, f"suf{t}")
                dve.tensor_tensor(cols(t, UK, NB), cols(t, UK, NB), ex[:, t, :], ALU.mult).then_inc(sem("ktail_done"), 1)
            elif step == ("mix_v", 0, 5):
                dve.wait_ge(sem("scores_cleared"), 1)
                mask = const("causal").unsqueeze(1).to_broadcast([P, GH, P]).bitcast(I32)
                for t in range(TT):
                    release(dve.copy_predicated(scm[:, t, :].rearrange("p (a b) -> p a b", a=GH), mask,
                                                take(dve, f"sc{t}")[:, :].rearrange("p (a b) -> p a b", a=GH)), f"sc{t}")
            elif stage == "mix_gate" and k == 0 and c in (1, 2, 4):
                n = (1, 2, 4).index(c)
                for j in range(2):
                    b = take(dve, f"kv{n}{j}")
                    if n == 0:
                        ins = dve.tensor_copy(state[:, 0, j * NB:(j + 1) * NB], b[:, :])
                    else:
                        wait_freed(dve, f"kv{n - 1}{j}")
                        t, half = n // 2, n % 2
                        for hd in (2 * j, 2 * j + 1):
                            end = hd * P + half * CHUNK + CHUNK - 1
                            v_ = slice(hd * GDV, (hd + 1) * GDV)
                            ins = dve.scalar_tensor_tensor(state[:, n, v_], state[:, n - 1, v_], up[:, t, end:end + 1],
                                                           b[:, (hd % 2) * GDV:(hd % 2 + 1) * GDV], ALU.mult, ALU.add)
                    release(ins, f"kv{n}{j}")
            elif stage == "mix_gate" and k == 1 and c >= 4:
                dve.wait_ge(sem("pool_split_hi"), c - 3)
                kt = 2 * (c - 4)
                dve.tensor_tensor(pair_lo["P"][:, kt:kt + 2, :], aq["pool_out"][:, kt:kt + 2, :],
                                  pair_hi["P"][:, kt:kt + 2, :].bitcast(F32), ALU.subtract).then_inc(sem("pool_split"), 1)
            elif step == ("mix_gate", 1, 1):
                dve.wait_ge(sem("head_root"), 1)
                link(dve.reciprocal(orstd, ostd))
                gla_heads_out(dve, 0)

        AK, AV, AI = 2048, 2560, 3072

        def group_of(first, gate, stage, k):
            if stage == first and k:
                return k - 1
            return KVH - 1 if stage == gate and k == 0 else None

        def index_use(n):
            return n // 8, n % 8 // 2 * 2, n % 2

        def index_step(stage, k, c):
            i = k * CH + c - 4 if stage == "a_kv" and c >= 0 else -1
            return range(2 * i, 2 * i + 2) if 0 <= i < 8 else ()

        def attention_a_pe(pe, stage, k, c):
            proj, kt_, ikt = ap["a_proj"], ae["kt_a"], ae["ikt"]
            g = group_of("a_q", "a_gate", stage, k)
            step = (stage, k, c)
            if step == ("a_kv", 0, 0):
                pe.wait_ge(acc_free, by_name["a_tail"].a0 + 1 + FREE0)
                narrow_back(pe, ikt, 80, "tail")
            if step == ("a_kv", 0, 3):
                pe.wait_ge(sem("index_rotated"), 1)
                b = use("ik")
                for t in range(TT):
                    ins = pe.transpose(b[:, t * P:(t + 1) * P], ae["ikd"][:, t, :], ident)
                filled(ins, "ik")
            if stage == "a_kv" and k == 0 and c in (3, 4):
                for name in (("iq00", "iq01", "iq10"), ("iq11",))[c - 3]:
                    t, j = int(name[2]), int(name[3])
                    b = use(name)
                    for i in range(4):
                        x = AI + (4 * j + i) * P
                        ins = pe.transpose(b[:, i * P:(i + 1) * P], proj[:, t, x:x + P], ident)
                    filled(ins, name)
            for n in index_step(stage, k, c):
                t, pair0, half = index_use(n)
                S = P * (t + 1)
                if n == 0:
                    wait_freed(pe, "ik")
                wait_freed(pe, f"iq{t}{pair0 // 4}")
                b = use(f"x{n}")
                rows = slice(half * ID, (half + 1) * ID)
                for i in range(2):
                    x = AI + (pair0 + i) * P
                    ins = pe.matmul(b[:, i * S:(i + 1) * S], proj[rows, t, x:x + P], ikt[rows, 0:S], start=True, stop=True)
                filled(ins, f"x{n}")
            if step == ("a_q", 0, 5):
                pe.wait_ge(sem("head_rotation_step"), 2 * TT)
                for t in range(TT):
                    b = use(f"ka{t}")
                    for i in range(4):
                        ins = pe.transpose(b[:, i * P:(i + 1) * P], proj[:, t, AK + i * P:AK + (i + 1) * P], ident)
                    filled(ins, f"ka{t}")
            if g is None:
                return
            if c == 1:
                for t in range(TT):
                    pe.wait_ge(sem("head_rotation_step"), 2 * TT * (g + 1) + 2 * (t + 1))
                    b = use(f"qa{t}_{g}")
                    for i in range(4):
                        ins = pe.transpose(b[:, i * P:(i + 1) * P], proj[:, t, g * NB + i * P:g * NB + (i + 1) * P], ident)
                    filled(ins, f"qa{t}_{g}")
            if c == 2:
                for t in range(TT):
                    wait_freed(pe, f"ka{t}")
                for t, name, i0, n in ((0, "l0", 0, 4), (1, "l10", 0, 2), (1, "l11", 2, 2)):
                    wait_freed(pe, f"qa{t}_{g}")
                    S = P * (t + 1)
                    b = use(f"{name}_{g}")
                    for i in range(n):
                        x = g * NB + (i0 + i) * P
                        ins = pe.matmul(b[:, i * S:(i + 1) * S], proj[:, t, x:x + P], kt_[:, g, 0:S], start=True, stop=True)
                    filled(ins, f"{name}_{g}")
            if c in (5, 6):
                for t, name, st in (((0, "pt0", 0),), ((1, "pt10", 0), (1, "pt11", 1)))[c - 5]:
                    pe.wait_ge(sem("exp_done"), 2 * g + t + 1)
                    b = use(f"{name}_{g}")
                    for i in range(4):
                        ins = pe.transpose(b[:, i * P:(i + 1) * P], ab[f"prob{t}"][:, i, st * P:(st + 1) * P], ident)
                    filled(ins, f"{name}_{g}")
            if c == 7:
                for t, names in ((0, ("pt0",)), (1, ("pt10", "pt11"))):
                    for name in names:
                        wait_freed(pe, f"{name}_{g}")
                    b = use(f"oa{t}_{g}")
                    for i in range(4):
                        for st in range(t + 1):
                            ins = pe.matmul(b[:, i * P:(i + 1) * P], ab["probt"][:, t + st, i * P:(i + 1) * P],
                                            proj[:, st, AV + g * P:AV + (g + 1) * P], start=(st == 0), stop=(st == t))
                    filled(ins, f"oa{t}_{g}")

        def attention_a_act(act, stage, k, c):
            proj = ap["a_proj"]
            g = group_of("a_q", "a_gate", stage, k)
            step = (stage, k, c)
            if step == ("a_kv", 0, 0):
                narrow_normed(act, ae["index_tail"], 80, "tail")
            if step == ("a_kv", 0, 3):
                release(act.copy(ae["ikt"][:, :], take(act, "ik")[:, 0:SEQ]), "ik")
            if stage == "a_kv" and k == 0 and c in (3, 4):
                for name in (("iq00", "iq01", "iq10"), ("iq11",))[c - 3]:
                    t, j = int(name[2]), int(name[3])
                    release(act.copy(proj[:, t, AI + j * NB:AI + (j + 1) * NB], take(act, name)[:, :]), name)
            for n in index_step(stage, k, c):
                S = P * (n // 8 + 1)
                b = take(act, f"x{n}")
                if n >= 2:
                    act.wait_ge(sem("relu_used"), n - 1)
                release(act.activation(sgw[:, n % 2, 0:2 * S], b[:, 0:2 * S], ACT.Relu), f"x{n}")
            if step == ("a_q", 0, 5):
                for t in range(TT):
                    release(act.copy(ae["kt_a"][:, :, t * P:(t + 1) * P], take(act, f"ka{t}")[:, :].rearrange("p (a n) -> p a n", a=4)), f"ka{t}")
            if g is None:
                return
            if c == 1:
                for t in range(TT):
                    release(act.copy(proj[:, t, g * NB:(g + 1) * NB], take(act, f"qa{t}_{g}")[:, :]), f"qa{t}_{g}")
            if c in (2, 3):
                t = c - 2
                act.wait_ge(sem("max_done"), 2 * g + t + 1)
                for i in range(4):
                    pr = ab[f"prob{t}"][:, i, :]
                    ins = act.activation(pr, pr, ACT.Exp, bias=nmax[:, t, i:i + 1], accum_out=rsum[:, 2 * g + t, i:i + 1])
                ins.then_inc(sem("exp_done"), 1)
            if c in (5, 6):
                for i, name in (((0, "pt0"),), ((1, "pt10"), (2, "pt11")))[c - 5]:
                    release(act.copy(ab["probt"][:, i, :], take(act, f"{name}_{g}")[:, :]), f"{name}_{g}")

        rotated = dict(head_rotation=0, index_rotation=0)

        def rotate(eng, view, heads, half, c0, tmp, tag):
            for t in range(TT):
                x1, x2 = view[t][:, :, 0:half], view[t][:, :, half:2 * half]
                cos = trig[:, 5, t, c0:c0 + half].unsqueeze(1).to_broadcast([P, heads, half])
                sin = trig[:, 3, t, c0:c0 + half].unsqueeze(1).to_broadcast([P, heads, half])
                part = [tmp[:, i, 0:heads * half].rearrange("p (a b) -> p a b", a=heads) for i in range(4)]
                for dst, x, f in zip(part, (x1, x2, x1, x2), (cos, sin, sin, cos)):
                    ins = eng.tensor_tensor(dst, x, f, ALU.mult)
                rotated[tag] += 1
                ins.then_inc(sem(f"{tag}_step"), 1)
                eng.wait_ge(sem(f"{tag}_step"), rotated[tag])
                eng.tensor_tensor(x1, part[0], part[1], ALU.subtract)
                rotated[tag] += 1
                eng.tensor_tensor(x2, part[2], part[3], ALU.add).then_inc(sem(f"{tag}_step"), 1)
                eng.wait_ge(sem(f"{tag}_step"), rotated[tag])

        def mixer_a_pool(pool):
            tail, proj = ae["index_tail"], ap["a_proj"]
            pool.wait_ge(acc_free, by_name["a_index"].a0 + 2 + FREE0)
            pool.wait_ge(sem("cos_done"), 1)
            view = [proj[:, t, AI:AI + IH * ID].rearrange("p (a b) -> p a b", a=IH) for t in range(TT)]
            rotate(pool, view, IH, IROT, ROT, ae["rope_b"], "index_rotation")
            wait_freed(pool, "tail")
            view = [tail[:, t, 0:ID].rearrange("p (a b) -> p a b", a=1) for t in range(TT)]
            rotate(pool, view, 1, IROT, ROT, ae["rope_b"], "index_rotation")
            for t in range(TT):
                for j in range(2):
                    ins = pool.tensor_copy(ae["ikd"][:, t, j * ID:(j + 1) * ID], tail[:, t, 0:ID])
            ins.then_inc(sem("index_rotated"), 1)
            for t in range(TT):
                pool.wait_ge(sem("relu_used"), 8 * (t + 1))
                diag = ae["isc"][:, t, t * P:(t + 1) * P]
                pool.affine_select(out=diag, in_=diag, pattern=[[-1, P]], compare_op=ALU.is_ge, fill=FAR, base=0,
                                   channel_multiplier=1).then_inc(sem("index_masked"), 1)

        def attention_a_dve(dve, link, stage, k, c):
            tail, isc, work, am, proj = ae["index_tail"], ae["isc"], ae["iwork"], ae["amask"], ap["a_proj"]
            g = group_of("a_q", "a_gate", stage, k)
            step = (stage, k, c)
            if step == ("a_index", 0, 0):
                dve.wait_ge(sem("trig_done"), 1)
                link(dve.tensor_tensor(trig[:, 5, :, :], trig[:, 4, :, :], trig[:, 4, :, :], ALU.mult))
                dve.tensor_scalar(trig[:, 5, :, :], trig[:, 5, :, :], -2.0, 1.0, ALU.mult, ALU.add).then_inc(sem("cos_done"), 1)
                dve.wait_ge(sem("cos_done"), 1)
            if step == ("a_kv", 0, 0):
                wait_freed(dve, "tail")
                iw = tail[:, :, ID:ID + IH]
                link(dve.tensor_scalar(iw, iw, float(ID) ** -0.5 * float(IH) ** -0.5, None, ALU.mult))
            if stage == "a_kv" and k == 0 and c in (0, 1):
                dve.wait_ge(sem("final_in"), 16)
                dve.scalar_tensor_tensor(h[:, c, :], h[:, c, :], rstd[:, c:c + 1], bc[:, 0, :], ALU.mult, ALU.mult).then_inc(sem("residual_done"), 1)
            for n in index_step(stage, k, c):
                t, pair0, half = index_use(n)
                S = P * (t + 1)
                wait_freed(dve, f"x{n}")
                for i in range(2):
                    hd = 2 * (pair0 + i) + half
                    rl, w_ = sgw[:, n % 2, i * S:(i + 1) * S], tail[:, t, ID + hd:ID + hd + 1]
                    if n % 8 == i == 0:
                        ins = dve.tensor_scalar(isc[:, t, 0:S], rl, w_, None, ALU.mult)
                    else:
                        ins = dve.scalar_tensor_tensor(isc[:, t, 0:S], rl, w_, isc[:, t, 0:S], ALU.mult, ALU.add)
                    if i == 0:
                        link(ins)
                ins.then_inc(sem("relu_used"), 1)
                dve.wait_ge(sem("relu_used"), n + 1)
            turns = {("a_kv", 1, 1): (0, range(0, 4)), ("a_kv", 1, 3): (0, range(4, 8)), ("a_kv", 1, 5): (1, range(0, 3)),
                     ("a_kv", 1, 6): (1, range(3, 6)), ("a_kv", 1, 7): (1, range(6, 8))}.get(step)
            if turns:
                t = turns[0]
                S = P * (t + 1)
                for n in turns[1]:
                    if n == 0:
                        dve.wait_ge(sem("index_masked"), t + 1)
                    src = work[:, t, 0:S] if n else isc[:, t, 0:S]
                    link(dve.max(top8, src))
                    link(dve.match_replace(work[:, t, 0:S], top8, src, TAKEN))
                if n == NSEL // 8 - 1:
                    link(dve.tensor_tensor(work[:, t, 0:S], work[:, t, 0:S], isc[:, t, 0:S], ALU.is_lt))
                    link(dve.scalar_tensor_tensor(work[:, t, 0:S], isc[:, t, 0:S], FAR * 0.5, work[:, t, 0:S], ALU.is_gt, ALU.mult))
                    link(dve.tensor_scalar(am[:, t, 0:S], work[:, t, 0:S], 1.0, 1.0e30, ALU.subtract, ALU.mult))
            if step == ("a_q", 0, 0):
                dve.wait_ge(acc_free, by_name["a_kv"].a0 + 2 + FREE0)
                view = [proj[:, t, AK:AK + NB].rearrange("p (a b) -> p a b", a=4) for t in range(TT)]
                rotate(dve, view, 4, ROT, 0, ae["rope_a"], "head_rotation")
            if g is None:
                return
            if c == -1:
                dve.wait_ge(acc_free, by_name["a_q"].a0 + g + 1 + FREE0)
                view = [proj[:, t, g * NB:(g + 1) * NB].rearrange("p (a b) -> p a b", a=4) for t in range(TT)]
                rotate(dve, view, 4, ROT, 0, ae["rope_a"], "head_rotation")
            if c in (2, 3):
                t = c - 2
                S, per = P * (t + 1), 4 // (t + 1)
                names = (("l0",), ("l10", "l11"))[t]
                if t == 0 and g == 0:
                    dve.wait_ge(sem("residual_done"), 2)
                for j, name in enumerate(names):
                    b = take(dve, f"{name}_{g}")
                    mask = am[:, t, 0:S].unsqueeze(1).to_broadcast([P, per, S])
                    ins = dve.scalar_tensor_tensor(ab[f"prob{t}"][:, j * per:(j + 1) * per, :],
                                                   b[:, 0:per * S].rearrange("p (a b) -> p a b", a=per), float(HD) ** -0.5, mask,
                                                   ALU.mult, ALU.add)
                    release(ins, f"{name}_{g}")
                wait_freed(dve, f"{names[-1]}_{g}")
                dve.tensor_reduce(nmax[:, t, :], ab[f"prob{t}"][:, :, :], AX.X, ALU.max, negate=True).then_inc(sem("max_done"), 1)
            if c == 7:
                for t in range(TT):
                    dve.wait_ge(sem("exp_done"), 2 * g + t + 1)
                    r_ = rsum[:, 2 * g + t, :]
                    link(dve.reciprocal(r_, r_))
                    b = take(dve, f"oa{t}_{g}")
                    release(dve.tensor_tensor(tm[:, t, g * NB:(g + 1) * NB].rearrange("p (a b) -> p a b", a=4),
                                              b[:, :].rearrange("p (a b) -> p a b", a=4),
                                              r_.unsqueeze(2).to_broadcast([P, 4, P]), ALU.mult), f"oa{t}_{g}")

        PAIRS = ((0, 0), (1, 0), (1, 1))
        BK, BV = 2048, 2560

        def unit(i):
            places = [aq["unit_q"][:, n, :] for n in range(4)] + [ae["unit_e"][:, n, :] for n in range(5)]
            return places[3 * i:3 * i + 3]

        def last_group(stage, k):
            if stage == "b_gate" and k < 2:
                return KVH - 2 + k
            return k - 2 if stage == "b_q" and k >= 2 else None

        def attention_b_pe(pe, stage, k, c):
            proj = aq["b_proj"]
            g, before = group_of("b_q", "b_gate", stage, k), last_group(stage, k)
            if (stage, k, c) == ("b_q", 0, 1):
                pe.wait_ge(acc_free, by_name["b_kv"].a0 + 2 + FREE0)
                for t in range(TT):
                    b = use(f"kb{t}")
                    for i in range(4):
                        ins = pe.transpose(b[:, i * P:(i + 1) * P], proj[:, t, BK + i * P:BK + (i + 1) * P], ident)
                    filled(ins, f"kb{t}")
            if before is not None and c == 2:
                pe.wait_ge(sem("weights_masked"), 2 * before + 2)
                pe.wait_ge(sem("stick_exp"), 3 * before + 3)
                for t in range(TT):
                    b = use(f"ob{t}_{before}")
                    for i in range(4):
                        for st in range(t + 1):
                            ins = pe.matmul(b[:, i * P:(i + 1) * P], unit(t + st)[2][:, i * P:(i + 1) * P],
                                            proj[:, st, BV + before * P:BV + (before + 1) * P], start=(st == 0), stop=(st == t))
                    filled(ins, f"ob{t}_{before}")
            if g is None:
                return
            if c == 1:
                pe.wait_ge(acc_free, by_name["b_q"].a0 + g + 1 + FREE0)
                for t in range(TT):
                    b = use(f"qb{t}_{g}")
                    for i in range(4):
                        ins = pe.transpose(b[:, i * P:(i + 1) * P], proj[:, t, g * NB + i * P:g * NB + (i + 1) * P], ident)
                    filled(ins, f"qb{t}_{g}")
            if c in (2, 3):
                for i in ((0, 1), (2,))[c - 2]:
                    t, st = PAIRS[i]
                    wait_freed(pe, f"kb{st}")
                    wait_freed(pe, f"qb{t}_{g}")
                    filled(pe.matmul(use(f"zb{i}_{g}")[:, :], proj[:, st, BK + g * P:BK + (g + 1) * P],
                                     proj[:, t, g * NB:(g + 1) * NB], start=True, stop=True), f"zb{i}_{g}")
            if c == 7:
                pe.wait_ge(sem("softplus_masked"), 2 * g + 2)
                wait_freed(pe, f"zb1_{g}")
                summed = [unit(0)[0], unit(1)[1], unit(2)[0]]
                for i in range(3):
                    b = use(f"fb{i}_{g}")
                    ins = pe.matmul(b[:, :], const("ntri"), summed[i], start=True, stop=(i != 1))
                    if i == 1:
                        ins = pe.matmul(b[:, :], const("nones"), summed[2], start=False, stop=True)
                    filled(ins, f"fb{i}_{g}")

        def attention_b_act(act, stage, k, c):
            proj = aq["b_proj"]
            g, before = group_of("b_q", "b_gate", stage, k), last_group(stage, k)
            if before is not None and c == 0:
                for i in range(3):
                    wait_freed(act, f"fb{i}_{before}")
                    x = unit(i)[2]
                    act.activation(x, x, ACT.Exp).then_inc(sem("stick_exp"), 1)
            if (stage, k, c) == ("b_q", 0, 1):
                for t in range(TT):
                    release(act.copy(proj[:, t, BK:BK + NB], take(act, f"kb{t}")[:, :]), f"kb{t}")
            if g is None:
                return
            if c == 1:
                for t in range(TT):
                    release(act.activation(proj[:, t, g * NB:(g + 1) * NB], take(act, f"qb{t}_{g}")[:, :], ACT.Copy,
                                           scale=float(HD) ** -0.5), f"qb{t}_{g}")
                act.preload_act_table_set("natural_log_exp_and_others")
            if c in (2, 3):
                for i in ((0, 1), (2,))[c - 2]:
                    n = 3 * (3 * g + i)
                    a_ = unit(i)[0]
                    b = take(act, f"zb{i}_{g}")
                    for func, src, scale, bias in ((ACT.Abs, b[:, :], 1.0, 0.0), (ACT.Exp, a_, -1.0, 0.0), (ACT.Ln, a_, 1.0, 1.0)):
                        act.activation(a_, src, func, scale=scale, bias=bias).then_inc(sem("stick_log"), 1)
                        n += 1
                        act.wait_ge(sem("stick_log"), n)

        def attention_b_dve(dve, link, stage, k, c):
            g, before = group_of("b_q", "b_gate", stage, k), last_group(stage, k)
            if before is not None and c == 2:
                for t in range(TT):
                    release(dve.tensor_copy(tm[:, t, before * NB:(before + 1) * NB], take(dve, f"ob{t}_{before}")[:, :]), f"ob{t}_{before}")
            if g is None:
                return
            if c in (3, 4):
                for i in ((0, 1), (2,))[c - 3]:
                    lo_, sp_, x = unit(i)
                    dve.wait_ge(sem("stick_log"), 3 * (3 * g + i) + 3)
                    b = take(dve, f"zb{i}_{g}")
                    link(dve.scalar_tensor_tensor(sp_, b[:, :], 0.0, lo_, ALU.max, ALU.add))
                    release(dve.tensor_tensor(x, b[:, :], sp_, ALU.subtract), f"zb{i}_{g}")
            if c == 7:
                for i in range(3):
                    x = unit(i)[2]
                    release(dve.tensor_tensor(x, x, take(dve, f"fb{i}_{g}")[:, :], ALU.add), f"fb{i}_{g}")

        def mixer_b_pool(pool):
            strict = const("strict").unsqueeze(1).to_broadcast([P, 4, P])

            def masked(dst, src, what):
                pool.tensor_tensor(dst.rearrange("p (a b) -> p a b", a=4), src.rearrange("p (a b) -> p a b", a=4),
                                   strict, ALU.mult).then_inc(sem(what), 1)

            for g in range(KVH):
                for i in (0, 2):
                    wait_freed(pool, f"zb{i}_{g}")
                    lo_, sp_, _ = unit(i)
                    masked(lo_, sp_, "softplus_masked")
                for i in (0, 2):
                    pool.wait_ge(sem("stick_exp"), 3 * g + i + 1)
                    x = unit(i)[2]
                    masked(x, x, "weights_masked")

        def beside_pe(pe, stage, k, c):
            if (stage, k, c) == ("ffn1_in0", 0, 7):
                pe.wait_ge(sem("vrow_in"), 80)
                filled(pe.transpose(use("gains")[:, 0:GAINS], vrow[0:GAINS, :], ident[0:GAINS, 0:GAINS]), "gains")
            gla_pe(pe, stage, k, c)
            attention_a_pe(pe, stage, k, c)
            attention_b_pe(pe, stage, k, c)

        def beside_act(act, stage, k, c):
            if (stage, k, c) == ("ffn1_in0", 0, 7):
                release(act.copy(vec[:, KT:GAINS], take(act, "gains")[:, KT:GAINS]), "gains")
                wait_freed(act, "gains")
            gla_act(act, stage, k, c)
            attention_a_act(act, stage, k, c)
            attention_b_act(act, stage, k, c)

        def beside_dve(dve, link, stage, k, c):
            if (stage, k, c) == ("ffn1_in0", 0, 7):
                wait_freed(dve, "gains")
                dve.memset(vrow[:, :], 1.0).then_inc(sem("ones_done"), 1)
            gla_dve(dve, link, stage, k, c)
            attention_a_dve(dve, link, stage, k, c)
            attention_b_dve(dve, link, stage, k, c)

        def gain_rows(eng, name, row, what):
            v = A[name] if len(A[name].shape) == 1 else A[name].rearrange("a n -> (a n)")
            v = v.rearrange("(r n) -> r n", n=P)
            eng.dma_start(vrow[row:row + v.shape[0], :], v).then_inc(sem(what), 16)

        block = ctx.enter_context(nc.Block())

        @block.sync
        def _(sp):
            xv = A["x"].rearrange("a (t p) n -> p (a t) n", p=P)
            for s in stages:
                w, k0, n0 = s.weights

                def load(k, u):
                    for c in range(CH):
                        tiles = s.chunk_tiles(c)
                        lo, n = k0 + tiles[0] * P, len(tiles) * P
                        if s is stages[0] and isinstance(k, int) and k == 0 and c % 2 == 0:
                            x_ = slice(c // 2 * NB, (c // 2 + 1) * NB)
                            sp.dma_start(h[:, :, x_], xv[:, :, x_]).then_inc(sem(f"x_in_{c // 2}"), 16)
                        sp.wait_ge(lo_done, (s.r0 + k) * CH + (c + 1))
                        col = n0 + (c // 2) * NB if s.kind == "ple" else n0 + k * NB
                        for i in range(2):
                            if s.kind == "ffn_in":
                                src = w[lo:lo + n, i, bass.ds(n0 + k * HB, HB)].rearrange("(j p) f -> p j f", p=P)
                                dst = raw[:, c, 0:2, i * HB:(i + 1) * HB]
                            elif len(tiles) == 2:
                                src = w[lo + i * P:lo + (i + 1) * P, bass.ds(col, s.width)]
                                dst = raw[:, c, i, 0:s.width]
                            else:
                                src = w[lo:lo + P, bass.ds(col + i * HB, HB)]
                                dst = raw[:, c, 0, i * HB:(i + 1) * HB]
                            sp.dma_start(dst, src).then_inc(landed[c], 16)

                paired_rounds(sp, s, load)
            view = out.rearrange("a (t p) n -> p (a t) n", p=P)
            for k in range(4):
                if last.kind == "gate":
                    sp.wait_ge(acc_free, FREE0 + last.a0 + k + 1)
                elif k == 0:
                    sp.wait_ge(acc_free, FREE0 + a)
                sp.dma_start(view[:, :, k * NB:(k + 1) * NB], h[:, :, k * NB:(k + 1) * NB]).then_inc(sem("stored"), 16)
            sp.wait_ge(sem("stored"), 64)

        @block.gpsimd
        def _(pool):
            for name, row in (("mix_norm", 16), ("ffn2_norm", 32), ("final_norm", 48), ("pool_scale", 64), ("gla_norm", 72)):
                gain_rows(pool, name, row, "vrow_in")
            pool.dma_start(con[:, P:], A["consts"][:, P:]).then_inc(const_in, 16)
            pool.dma_start(posi[:, :], A["positions_2"].rearrange("a (t p) -> p (a t)", p=P),
                           allow_slow_non_contiguous=True).then_inc(sem("pos_in"), 16)
            pool.dma_start(ab["walpha"][0:16, :], A["w_alpha"]).then_inc(sem("pool_in"), 16)
            pool.dma_start(ab["balpha"][0:1, :], A["b_alpha"]).then_inc(sem("pool_in"), 16)
            pool.dma_start(ae["band"][:, :, :, :], A["band"]).then_inc(sem("pool_in"), 16)
            pool.dma_start(ae["wpool"][:, :, :, :], A["w_pool"].rearrange("g (c p) d -> p g c d", p=P)).then_inc(sem("pool_in"), 16)
            if "a_index" in by_name:
                pool.wait_ge(chunk_used, by_name["mix_out"].r0 * CH + 1 + USED0)
                pool.dma_start(bc[:, 0, :], A["final_norm"].partition_broadcast(P)).then_inc(sem("final_in"), 16)
            if "a_kv" in by_name:
                mixer_a_pool(pool)
            for i, nm in enumerate(("a_out", "b_out")):
                if nm not in by_name:
                    continue
                attention_done(pool, nm)
                pool.dma_start(ae["ptm"][:, :, :], A["p_2"][i].rearrange("a (t p) n -> p (a t) n", p=P)).then_inc(sem("p_in"), 16)
                pool.dma_start(bc[:, 0, :], A["ln_g_2"][i].partition_broadcast(P)).then_inc(sem(f"ln_in_{i}"), 16)
                pool.dma_start(bc[:, 1, :], A["ln_b_2"][i].partition_broadcast(P)).then_inc(sem(f"ln_in_{i}"), 16)
                if i == 0 and "b_kv" in by_name:
                    mixer_b_pool(pool)

        @block.tensor
        def _(pe):
            pe.sem_inc(chunk_used, USED0)

            def transposes(s, b, u):
                number, parity, pair, kt, gain = resolve(s, b, u)
                dst = bank[4 + parity]
                if isinstance(b, Batch):
                    issued[0] = number + 1
                if not isinstance(b, Batch) or number >= 2:
                    pe.wait_ge(t_done, number - 1)
                if emitted[4 + parity]:
                    pe.wait_ge(freed_s[4 + parity], emitted[4 + parity])
                if isinstance(b, tuple):
                    pe.wait_ge(acc_free, s.a0 + b[1] + FREE0)
                    src = [hid[:, (u - 1) % 2, t, j * P:(j + 1) * P] for j in range(2) for t in range(TT)]
                elif isinstance(b.source, tuple):
                    pe.wait_ge(acc_free, s.a0 + FREE0)
                    src = [hid[:, b.source[0], t, j * P:(j + 1) * P] for j in range(2) for t in range(TT)]
                else:
                    src = b.source(kt)
                for n, piece in enumerate(src):
                    ins = pe.transpose(dst[:, n * P:(n + 1) * P], piece, ident)
                ins.then_inc(t_full, 1)

            def source_wait(s, b):
                if s.name == "mix_out":
                    for t in range(TT):
                        wait_freed(pe, f"og{t}{b.kt // 4 - 2}")
                elif b.kt % 4 == 0:
                    if s.kind in ("ple", "gate"):
                        pe.wait_ge(sem(f"normed_{s.name[-1]}"), b.kt // 4 + 1)
                    else:
                        pe.wait_ge(sem(f"x_in_{b.kt // 4}"), 16)

            def middle_wait(s, k):
                pe.wait_ge(acc_free, s.a0 + k + FREE0)
                if s.kind == "ln_out" and k == 1:
                    pe.wait_ge(sem("p_in"), 16 * (1 if s.name == "a_out" else 2))

            def multiply(s, k, u, c, dst, t_first, t_last):
                tiles = s.chunk_tiles(c)
                pe.wait_ge(lo_done, (s.r0 + k) * CH + (c + 1 + LO0))
                xh, xl = pair_hi[s.pair], pair_lo[s.pair]
                for j, kt in enumerate(tiles):
                    for t in range(TT):
                        o = dst[t][:, 0:s.width]
                        wh, wl = whi[:, c % SPLIT, j, 0:s.width], wlo[:, c % SPLIT, j, 0:s.width]
                        if s.kind == "narrow":
                            if t:
                                continue
                            o = dst[0][0:s.width, 0:SEQ]
                            pe.matmul(o, wh, xh[:, kt, :], start=(kt == t_first), stop=False)
                            pe.matmul(o, wl, xh[:, kt, :], start=False, stop=False)
                            ins = pe.matmul(o, wh, xl[:, kt, :], start=False, stop=(kt == t_last))
                            continue
                        xht, xlt = xh[:, kt, t * P:(t + 1) * P], xl[:, kt, t * P:(t + 1) * P]
                        pe.matmul(o, xht, wh, start=(kt == t_first), stop=False)
                        pe.matmul(o, xht, wl, start=False, stop=False)
                        ins = pe.matmul(o, xlt, wh, start=False, stop=(kt == t_last))
                return ins

            def prev_of(s):
                return stages[stages.index(s) - 1]

            pe.wait_ge(ident_in, 16)
            pe.wait_ge(sem("first_gain_in"), 16)
            filled(pe.transpose(use("vec")[:, 0:KT], vrow[0:KT, :], ident[0:KT, 0:KT]), "vec")
            for s in stages:
                for b in s.ahead:
                    source_wait(s, b)
                    transposes(s, b, 0)

                def round_(k, u):
                    peeled = isinstance(k, int)
                    if s.kind != "ple":
                        pe.wait_ge(acc_free, s.a0 + k + 1)
                    dst = [acc_par(s, u, t) for t in range(TT)]
                    tiles = [kt for c in range(CH) for kt in s.chunk_tiles(c)]
                    for c in range(CH):
                        for b in s.mid.get(c, []) if peeled and k == 0 else []:
                            source_wait(s, b)
                            transposes(s, b, u)
                        if c == 4:
                            todo = batches_of(s, k, peeled)
                            if peeled and s.before.get(k):
                                middle_wait(s, k)
                            for b in todo:
                                transposes(s, b, u)
                        if s.kind == "ple":
                            j = c // 2
                            dst = [acc(s.a0 + j, t) for t in range(TT)]
                            if c % 2 == 0:
                                pe.wait_ge(acc_free, s.a0 + j + 1)
                        if peeled and k == 0:
                            if s.name == "mix_out" and c < 4:
                                pe.wait_ge(sem("pool_split"), c + 1)
                            pe.wait_ge(t_done, s.need[c])
                        ins = multiply(s, k, u, c, dst, tiles[0], 1 if s.kind == "ple" else tiles[-1])
                        ins.then_inc(chunk_used, 1)
                        if peeled:
                            beside_pe(pe, s.name, k, c)

                paired_rounds(pe, s, round_)

        @block.scalar
        def _(act):
            act.dma_start(con[:, 0:P], A["consts"][:, 0:P]).then_inc(ident_in, 16)
            gain_rows(act, "ffn1_norm", 0, "first_gain_in")
            act.wait_ge(sem("cleared"), 1)
            act.copy(one_c, eps_c)

            def split_hi(s, k, c, n):
                act.wait_ge(landed[c], (s.r0 + k) * 32 + 32)
                act.wait_ge(chunk_used, (s.r0 + k) * CH + (c + 1))
                w = s.width
                act.copy(whi[:, c % SPLIT, 0:n, 0:w], raw[:, c, 0:n, 0:w]).then_inc(hi_done, 1)

            def operand_hi(s, b, u):
                number, parity, pair, kt, gain = resolve(s, b, u)
                act.wait_ge(t_full, number + 1)
                src = bank[4 + parity]
                dst = pair_hi[pair]
                if gain is None:
                    act.copy(dst[:, bass.ds(kt, 2), :], src[:, :].rearrange("p (j n) -> p j n", j=2)).then_inc(t_hi, 1)
                else:
                    for j in range(2):
                        g = GAIN["gla"] + j if gain == "gla" else gain + kt + j
                        ins = act.activation(dst[:, kt + j, :], src[:, j * SEQ:(j + 1) * SEQ], ACT.Copy, scale=vec[:, g:g + 1])
                    ins.then_inc(t_hi, 1)

            squared = [0]

            def squares(blk):
                if squared[0]:
                    act.wait_ge(sem("squares_done"), squared[0])
                squared[0] += 1
                for t in range(TT):
                    ins = act.activation(sgw[:, t, :], h[:, t, blk * NB:(blk + 1) * NB], ACT.Square,
                                         accum_out=parts[:, t, blk:blk + 1])
                ins.then_inc(sem("squares_done"), 1)

            def root(n):
                act.wait_ge(sem("sumsq_done"), n + 1)
                act.activation(std, ssq, ACT.Sqrt, bias=eps_c, scale=1.0 / D).then_inc(sem("root_done"), 1)
                act.wait_ge(sem("rstd_done"), n + 1)

            def evacuate(s, k, u):
                peeled = isinstance(k, int)
                pair = [acc_par(s, u, t) for t in range(TT)]
                full_at = s.a0 + k + 1
                if s.kind == "ffn_in":
                    sums_done(act, s, k)
                    for t in range(TT):
                        ins = act.activation(sg[:, u, t, :], pair[t][:, 0:HB], ACT.Silu, scale=rstd[:, t:t + 1])
                    ins.then_inc(silu_done, 1)
                elif s.name in ("ffn1_out2", "mix_out", "ffn2_out2"):
                    act.wait_ge(acc_free, full_at + FREE0)
                    squares(k)
                elif s.kind == "narrow":
                    sums_done(act, s, k)
                    w = s.width
                    act.copy((ab["rt"] if s.name == "mix_decay" else ae["ikt"])[0:w, :], pair[0][0:w, 0:SEQ]).then_inc(acc_free, 1)
                elif s.kind == "project":
                    sums_done(act, s, k)
                    width = s.width
                    for t in range(TT):
                        func, dst = placed(s, k, t)
                        scale = rstd[:, t:t + 1] if s.name[0] != "b" else 1.0
                        ins = act.activation(dst, pair[t][:, 0:width], func, scale=scale)
                    ins.then_inc(acc_free, 1)
                elif s.kind in ("gate", "head_gate"):
                    sums_done(act, s, k)
                    act.wait_ge(acc_free, full_at - 1 + FREE0)
                    for t in range(TT):
                        if s.kind == "gate":
                            ins = act.activation(sgw[:, t, :], pair[t][:, :], ACT.Sigmoid)
                        else:
                            ins = act.activation(sgw[:, t, :], pair[t][:, :], ACT.Silu,
                                                 scale=rstd[:, t:t + 1] if s.name[0] == "a" else 1.0)
                    ins.then_inc(silu_done, 1)

            def placed(s, k, t):
                if s.name == "mix_gate":
                    return ACT.Silu, tm[:, t, 1024 + k * NB:1024 + (k + 1) * NB]
                buf, first = dict(mix_pool=(aq["u"], 0), mix_qk=(aq["u"], 1024), mix_v=(aq["u"], 2048),
                                  a_index=(ap["a_proj"], 3072), a_kv=(ap["a_proj"], 2048), a_q=(ap["a_proj"], 0),
                                  b_kv=(aq["b_proj"], 2048), b_q=(aq["b_proj"], 0))[s.name]
                return ACT.Copy, buf[:, t, first + k * NB:first + (k + 1) * NB]

            def ple_out(s, j):
                act.wait_ge(chunk_used, s.r0 * CH + 2 * (j + 1) + USED0)
                for t in range(TT):
                    ins = act.copy(tm[:, t, j * NB:(j + 1) * NB], acc(s.a0 + j, t)[:, :])
                ins.then_inc(acc_free, 1)

            def first_half(s, k, peeled):
                for c in range(4):
                    split_hi(s, k, c, 1 if s.kind == "ple" else 2)
                    if s.kind == "gate" and isinstance(k, int) and k == 0 and c < 2:
                        ple_out(stages[stages.index(s) - 1], c + 2)
                    if isinstance(k, int) and k == 0:
                        for b in (s.ahead if c == 0 else []) + ([] if s.late else s.mid.get(c, [])):
                            operand_hi(s, b, 0)
                    if peeled and s.r0 + k:
                        beside_act(act, *round_before(s, k), c + 4)

            release(act.copy(vec[:, 0:KT], take(act, "vec")[:, 0:KT]), "vec")
            wait_freed(act, "vec")
            s0 = stages[0]
            first_half(s0, 0, True)
            for n, s in enumerate(stages):
                nxt = stages[n + 1] if n + 1 < len(stages) else None

                def second_half(k, u):
                    peeled = isinstance(k, int)
                    for b in s.mid[3] if s.late and peeled and k == 0 else []:
                        operand_hi(s, b, u)
                    for c in range(4, CH):
                        split_hi(s, k, c, 1 if s.kind == "ple" or s.tiles == 12 else 2)
                        for b in s.mid.get(c, []) if peeled and k == 0 else []:
                            operand_hi(s, b, u)
                        if s.kind == "ple" and c == 5:
                            act.wait_ge(sem("mean_var_done"), 1 if s.name == "ple0" else 2)
                            act.activation(std, mv[:, :, 1], ACT.Sqrt, bias=lneps_c).then_inc(sem("ln_root_done"), 1)
                        if s.kind == "ple" and c in (5, 7):
                            ple_out(s, c // 2 - 2)
                        if s is s0 and peeled and k == 0:
                            act.wait_ge(sem(f"x_in_{c - 4}"), 16)
                            squares(c - 4)
                        if peeled:
                            beside_act(act, s.name, k, c - 4)
                    for b in batches_of(s, k, peeled):
                        operand_hi(s, b, u)

                def round_(k, u):
                    peeled = isinstance(k, int)
                    second_half(k, u)
                    if not (peeled and k == s.n - 1):
                        first_half(s, k + 1, peeled)
                    elif nxt is not None:
                        first_half(nxt, 0, peeled)
                    if peeled and k == 0 and s.name in NORMED:
                        root(NORMED.index(s.name))
                    if s.kind != "ple":
                        evacuate(s, k, u)
                    if s is s0 and peeled and k == 1:
                        act.wait_ge(sem("trig_args"), 1)
                        act.activation(trig[:, 3, :, :], trig[:, 2, :, :], ACT.Sin)
                        act.activation(trig[:, 4, :, :], trig[:, 2, :, :], ACT.Sin, scale=0.5).then_inc(sem("trig_done"), 1)

                paired_rounds(act, s, round_)

        @block.vector
        def _(dve):
            dve.sem_inc(lo_done, LO0)
            dve.sem_inc(acc_free, FREE0)
            steps = sem("vector_step")
            stepped = [0]

            def link(ins):
                stepped[0] += 1
                ins.then_inc(steps, 1)
                dve.wait_ge(steps, stepped[0])

            def split_lo(s, k, c, n):
                dve.wait_ge(hi_done, (s.r0 + k) * CH + (c + 1))
                w = s.width
                dve.tensor_tensor(wlo[:, c % SPLIT, 0:n, 0:w], raw[:, c, 0:n, 0:w], whi[:, c % SPLIT, 0:n, 0:w].bitcast(F32),
                                  ALU.subtract).then_inc(lo_done, 1)

            def operand_lo(s, b, u):
                number, parity, pair, kt, gain = resolve(s, b, u)
                dve.wait_ge(t_hi, number + 1)
                src, hi_, lo_ = bank[4 + parity], pair_hi[pair], pair_lo[pair]
                if gain is None:
                    dve.tensor_tensor(lo_[:, bass.ds(kt, 2), :], src[:, :].rearrange("p (j n) -> p j n", j=2),
                                      hi_[:, bass.ds(kt, 2), :].bitcast(F32), ALU.subtract).then_inc(t_done, 1)
                else:
                    for j in range(2):
                        g = GAIN["gla"] + j if gain == "gla" else gain + kt + j
                        ins = dve.scalar_tensor_tensor(lo_[:, kt + j, :], src[:, j * SEQ:(j + 1) * SEQ], vec[:, g:g + 1],
                                                       hi_[:, kt + j, :].bitcast(F32), ALU.mult, ALU.subtract)
                    ins.then_inc(t_done, 1)

            def rms(n):
                dve.wait_ge(sem("squares_done"), 4 * n + 4)
                dve.tensor_reduce(ssq, parts, AX.X, ALU.add).then_inc(sem("sumsq_done"), 1)
                dve.wait_ge(sem("root_done"), n + 1)
                dve.reciprocal(rstd, std).then_inc(sem("rstd_done"), 1)
                dve.wait_ge(sem("rstd_done"), n + 1)

            def evacuate(s, k, u):
                pair = [acc_par(s, u, t) for t in range(TT)]
                at_ = s.a0 + k + 1
                if s.kind == "ffn_in":
                    dve.wait_ge(silu_done, silu_before(s) + k + 1)
                    for t in range(TT):
                        ins = dve.scalar_tensor_tensor(hid[:, u, t, :], pair[t][:, HB:NB], rstd[:, t:t + 1],
                                                       sg[:, u, t, :], ALU.mult, ALU.mult)
                    ins.then_inc(acc_free, 1)
                elif s.kind in ("ffn_out", "mix_out", "ln_out"):
                    sums_done(dve, s, k)
                    for t in range(TT):
                        hb = h[:, t, k * NB:(k + 1) * NB]
                        if s.kind == "ln_out":
                            ins = dve.scalar_tensor_tensor(hb, hb, ALPHA, pair[t][:, :], ALU.mult, ALU.add)
                        else:
                            c = 0.5 if s.kind == "ffn_out" else 1.0
                            ins = dve.scalar_tensor_tensor(hb, pair[t][:, :], c, hb, ALU.mult, ALU.add)
                    ins.then_inc(acc_free, 1)
                    if s.kind == "ln_out":
                        dve.wait_ge(acc_free, at_ + FREE0)
                        for t in range(TT):
                            ins = dve.bn_stats(bn[:, t, k, :], h[:, t, k * NB:(k + 1) * NB])
                        link(ins)
                elif s.kind == "head_gate":
                    dve.wait_ge(silu_done, silu_before(s) + k + 1)
                    for t in range(TT):
                        o = tm[:, t, k * NB:(k + 1) * NB]
                        ins = dve.tensor_tensor(o, o, sgw[:, t, :], ALU.mult)
                    ins.then_inc(acc_free, 1)
                elif s.kind == "gate":
                    dve.wait_ge(silu_done, silu_before(s) + k + 1)
                    for t in range(TT):
                        ins = dve.tensor_tensor(sgw[:, t, :], sgw[:, t, :], tm[:, t, k * NB:(k + 1) * NB], ALU.mult)
                    link(ins)
                    for t in range(TT):
                        hb = h[:, t, k * NB:(k + 1) * NB]
                        ins = dve.tensor_tensor(hb, hb, sgw[:, t, :], ALU.add)
                    ins.then_inc(acc_free, 1)

            def silu_before(s):
                return sum(q.n for q in stages[:stages.index(s)] if q.kind in ("ffn_in", "gate", "head_gate"))

            PLE, GATES = ("ple0", "ple1"), ("gate0", "gate1")

            def norm_block(i, k):
                cols = slice(k * NB, (k + 1) * NB)
                for t in range(TT):
                    ins = dve.scalar_tensor_tensor(h[:, t, cols], h[:, t, cols], mv[:, t, 0:1], bc[:, 0, cols],
                                                   ALU.subtract, ALU.mult)
                link(ins)
                for t in range(TT):
                    ins = dve.scalar_tensor_tensor(h[:, t, cols], h[:, t, cols], rstd[:, t:t + 1], bc[:, 1, cols],
                                                   ALU.mult, ALU.add)
                ins.then_inc(sem(f"normed_{i}"), 1)

            def layer_norm_start():
                link(dve.bn_aggr(mv[:, 0, :], bn[:, 0, :, :]))
                dve.bn_aggr(mv[:, 1, :], bn[:, 1, :, :]).then_inc(sem("mean_var_done"), 1)

            def layer_norm_root(i):
                dve.wait_ge(sem("ln_root_done"), i + 1)
                link(dve.reciprocal(rstd, std))
                dve.wait_ge(sem(f"ln_in_{i}"), 32)

            def first_half(s, k, peeled):
                for c in range(4):
                    if s.kind == "gate" and isinstance(k, int) and k == 0 and c in (1, 3):
                        norm_block(GATES.index(s.name), (c + 1) // 2)
                    split_lo(s, k, c, 1 if s.kind == "ple" else 2)
                    if isinstance(k, int) and k == 0:
                        for b in (s.ahead if c == 0 else []) + ([] if s.late else s.mid.get(c, [])):
                            operand_lo(s, b, 0)
                    if peeled and s.r0 + k:
                        beside_dve(dve, link, *round_before(s, k), c + 4)
                if s.kind == "gate" and isinstance(k, int) and k == 0:
                    norm_block(GATES.index(s.name), 3)

            dve.memset(eps_c, EPS)
            dve.memset(lneps_c, LN_EPS).then_inc(sem("cleared"), 1)
            s0 = stages[0]
            wait_freed(dve, "vec")
            first_half(s0, 0, True)
            for n, s in enumerate(stages):
                nxt = stages[n + 1] if n + 1 < len(stages) else None
                if s.name == "mix_out":
                    gla_heads_out(dve, 1)

                def round_(k, u):
                    peeled = isinstance(k, int)
                    if peeled:
                        beside_dve(dve, link, s.name, k, -1)
                    if s.kind == "ple":
                        layer_norm_start()
                    for b in s.mid[3] if s.late and peeled and k == 0 else []:
                        operand_lo(s, b, u)
                    for c in range(4, CH):
                        split_lo(s, k, c, 1 if s.kind == "ple" or s.tiles == 12 else 2)
                        for b in s.mid.get(c, []) if peeled and k == 0 else []:
                            operand_lo(s, b, u)
                        if s.kind == "ple" and c == 5:
                            layer_norm_root(PLE.index(s.name))
                            norm_block(PLE.index(s.name), 0)
                        if peeled:
                            beside_dve(dve, link, s.name, k, c - 4)
                    for b in batches_of(s, k, peeled):
                        operand_lo(s, b, u)
                    if not (peeled and k == s.n - 1):
                        first_half(s, k + 1, peeled)
                    elif nxt is not None:
                        first_half(nxt, 0, peeled)
                    if peeled and k == 0 and s.name in NORMED:
                        rms(NORMED.index(s.name))
                    evacuate(s, k, u)
                    if s is s0 and peeled and k == 0:
                        angles(dve, link)

                paired_rounds(dve, s, round_)
    return stages


_INS = ['x', 'ffn1_norm', 'ffn1_w_in', 'ffn1_w_out', 'mix_norm', 'w_in_mix', 'w_pool', 'pool_scale', 'w_alpha',
        'b_alpha', 'gla_norm', 'w_out_mix', 'ffn2_norm', 'ffn2_w_in', 'ffn2_w_out', 'final_norm', 'p_2',
        'positions_2', 'w_in_a_2', 'w_o_a_2', 'w_kv_b_2', 'w_in_b_2', 'w_o_b_2', 'ln_g_2', 'ln_b_2', 'w_ple_2',
        'w_ple_gate_2']
_ONE_LAYER = {'ffn1_w_in', 'ffn1_w_out', 'w_in_mix', 'w_pool', 'w_alpha', 'w_out_mix', 'ffn2_w_in', 'ffn2_w_out',
              'w_in_a_2', 'w_o_a_2', 'w_in_b_2', 'w_o_b_2'}


def kernel(**inputs):
    import numpy as _np
    import concourse.bacc as _bacc
    from concourse import mybir as _mybir
    from concourse.bass_utils import run_bass_kernel_spmd as _run

    nc = _bacc.Bacc("TRN2", target_bir_lowering=False, num_devices=1)
    given = {name: _np.ascontiguousarray(inputs[name]) for name in _INS}
    given["consts"], given["band"] = shape_constants()
    arrays, args = {}, {}
    for name, a in given.items():
        arrays[f"in_{name}_dram"] = a
        ap = nc.dram_tensor(f"in_{name}_dram", a.shape, _mybir.dt.from_np(a.dtype), kind="ExternalInput").ap()
        args[name] = ap[0] if name in _ONE_LAYER else ap
    out = nc.dram_tensor("out_0_dram", (1, SEQ, D), _mybir.dt.float32, kind="ExternalOutput").ap()
    build(nc, args, out)
    return _run(nc, [arrays], core_ids=[0]).results[0]["out_0_dram"]
```
